# Optimizing a Trainium2 kernel written in Bass

```python
import jax
import jax.numpy as jnp
from jax import lax
import numpy as np
import math
import jax, jax.numpy as jnp

D_MODEL = 1024
BATCH = 1
SEQ = 256
DEPTH = 2

CHUNK = 64
Q_BLOCK = 128
N_HEADS = 4
HEAD_DIM = 128
BRANCH_W = N_HEADS * HEAD_DIM
RET_DK = HEAD_DIM
RET_DV = HEAD_DIM
GLA_DK = HEAD_DIM // 2
GLA_DV = HEAD_DIM
GLA_LOWRANK = 16
GLA_TAU = 16.0
FOX_D = HEAD_DIM
N_BRANCH = 3
D_FF = 2816
CONV_W = 3
ROPE_BASE = 10000.0
EPS = 1e-6

IN_SPLITS = (
    N_HEADS * RET_DK, N_HEADS * RET_DK, N_HEADS * RET_DV, N_HEADS * RET_DV,
    N_HEADS * GLA_DK, N_HEADS * GLA_DK, N_HEADS * GLA_DV, GLA_LOWRANK, N_HEADS * GLA_DV,
    N_HEADS * FOX_D, N_HEADS * FOX_D, N_HEADS * FOX_D, N_HEADS,
)
IN_W = sum(IN_SPLITS)


F32 = jnp.float32

def rms_norm(x, g):
    xf = x.astype(F32)
    y = xf * lax.rsqrt(jnp.mean(xf * xf, axis=-1, keepdims=True) + EPS)
    return (y * g).astype(x.dtype)

def head_group_norm(x, g):
    xf = x.astype(F32)
    mu = jnp.mean(xf, axis=-1, keepdims=True)
    xc = xf - mu
    return xc * lax.rsqrt(jnp.mean(xc * xc, axis=-1, keepdims=True) + EPS) * g

def modulate(h, shift, scale):
    return h * (1.0 + scale[:, None, :]) + shift[:, None, :]

def rotary(x, pos):
    half = x.shape[-1] // 2
    inv_freq = ROPE_BASE ** (-jnp.arange(half, dtype=F32) / half)
    ang = pos[:, None] * inv_freq[None, :]
    cos = jnp.cos(ang)[None, :, None, :]
    sin = jnp.sin(ang)[None, :, None, :]
    x1, x2 = x[..., :half], x[..., half:]
    return jnp.concatenate([x1 * cos - x2 * sin, x1 * sin + x2 * cos], axis=-1)

def retention(q, k, v):
    b, s, h, dk = q.shape
    dv = v.shape[-1]
    n = s // CHUNK
    pos = jnp.arange(s, dtype=F32)
    q = rotary(q.astype(F32), pos)
    k = rotary(k.astype(F32), pos) * dk ** -0.5
    v = v.astype(F32)
    log_g = jnp.log1p(-jnp.exp2(-5.0 - jnp.arange(h, dtype=F32)))
    idx = jnp.arange(CHUNK, dtype=F32)
    d_intra = jnp.exp(jnp.abs(idx[:, None] - idx[None, :])[None] * log_g[:, None, None])
    qc = q.reshape(b, n, CHUNK, h, dk)
    kc = k.reshape(b, n, CHUNK, h, dk)
    vc = v.reshape(b, n, CHUNK, h, dv)
    scores = jnp.einsum('bnihd,bnjhd->bnhij', qc, kc) * d_intra
    o_intra = jnp.einsum('bnhij,bnjhe->bnihe', scores, vc)
    k_w = jnp.exp((CHUNK - 1.0 - idx)[:, None] * log_g[None, :])
    kv = jnp.einsum('bnjhd,bnjhe->nbhde', kc * k_w[:, :, None], vc)
    g_chunk = jnp.exp(CHUNK * log_g)[None, :, None, None]

    def step(r, kv_n):
        return g_chunk * r + kv_n, r

    _, r_prev = lax.scan(step, jnp.zeros((b, h, dk, dv), F32), kv)
    q_w = jnp.exp((idx + 1.0)[:, None] * log_g[None, :])
    o_cross = jnp.einsum('bnihd,nbhde->bnihe', qc * q_w[:, :, None], r_prev)
    return (o_intra + o_cross).reshape(b, s, h, dv)

def gla(q, k, v, log_a):
    b, s, h, dk = q.shape
    dv = v.shape[-1]
    n = s // CHUNK
    qc = (q.astype(F32) * dk ** -0.5).reshape(b, n, CHUNK, h, dk)
    kc = k.astype(F32).reshape(b, n, CHUNK, h, dk)
    vc = v.astype(F32).reshape(b, n, CHUNK, h, dv)
    la = log_a.astype(F32).reshape(b, n, CHUNK, h, dk)
    b_cum = jnp.cumsum(la, axis=2)
    b_end = b_cum[:, :, -1:]
    kv = jnp.einsum('bnjhd,bnjhe->nbhde', kc * jnp.exp(b_end - b_cum), vc)
    a = jnp.exp(b_end[:, :, 0]).transpose(1, 0, 2, 3)

    def step(st, inp):
        a_n, kv_n = inp
        st = a_n[..., None] * st + kv_n
        return st, st

    _, s_all = lax.scan(step, jnp.zeros((b, h, dk, dv), F32), (a, kv))
    o = jnp.einsum('bnihd,nbhde->bnihe', qc, s_all)
    return o.reshape(b, s, h, dv)

def forgetting_attention(q, k, v, f_logit):
    b, s, h, d = q.shape
    log_f = jax.nn.log_sigmoid(f_logit.astype(F32))
    cum = jnp.cumsum(log_f, axis=1).transpose(0, 2, 1)
    outs = []
    for blk in range(s // Q_BLOCK):
        q0 = blk * Q_BLOCK
        q1 = q0 + Q_BLOCK
        logits = jnp.einsum('bihd,bjhd->bhij', q[:, q0:q1], k[:, :q1]).astype(F32) * d ** -0.5
        logits = logits + cum[:, :, q0:q1, None] - cum[:, :, None, :q1]
        mask = jnp.arange(q0, q1)[:, None] >= jnp.arange(q1)[None, :]
        p = jax.nn.softmax(jnp.where(mask, logits, -jnp.inf), axis=-1).astype(v.dtype)
        outs.append(jnp.einsum('bhij,bjhe->bihe', p, v[:, :q1]))
    return jnp.concatenate(outs, axis=1)

def causal_dwconv(u, w, bias):
    s = u.shape[1]
    up = jnp.pad(u, ((0, 0), (CONV_W - 1, 0), (0, 0)))
    out = bias
    for j in range(CONV_W):
        out = out + w[j] * up[:, j:j + s]
    return out

def hybrid_layer(x, c_act, norm1_g, norm2_g, w_ada, b_ada, w_in, w_gla_a2, b_gla_a, b_fox_f,
                 ret_norm_g, gla_norm_g, q_norm_g, k_norm_g, w_br, w_mg, b_mg, w_o,
                 w_up, w_conv, b_conv, w_down):
    b, s = x.shape[0], x.shape[1]
    mod = c_act @ w_ada + b_ada
    shift1, scale1, gate1, shift2, scale2, gate2 = jnp.split(mod, 6, axis=-1)

    h = modulate(rms_norm(x, norm1_g), shift1, scale1)
    split_points = np.cumsum(IN_SPLITS)[:-1].tolist()
    (rq, rk, rv, rg, gq, gk, gv, glr, gg, fq, fk, fv, ff) = jnp.split(h @ w_in, split_points, axis=-1)

    def heads(t, d):
        return t.reshape(b, s, N_HEADS, d)

    ret = retention(heads(rq, RET_DK), heads(rk, RET_DK), heads(rv, RET_DV))
    ret = head_group_norm(ret, ret_norm_g.reshape(N_HEADS, RET_DV)).reshape(b, s, BRANCH_W)
    ret = jax.nn.silu(rg) * ret

    log_a = jax.nn.log_sigmoid((glr @ w_gla_a2 + b_gla_a).astype(F32)) / GLA_TAU
    gla_o = gla(heads(gq, GLA_DK), heads(gk, GLA_DK), heads(gv, GLA_DV), heads(log_a, GLA_DK))
    gla_o = rms_norm(gla_o, gla_norm_g).reshape(b, s, BRANCH_W)
    gla_o = jax.nn.silu(gg) * gla_o

    fox_o = forgetting_attention(rms_norm(heads(fq, FOX_D), q_norm_g),
                                 rms_norm(heads(fk, FOX_D), k_norm_g),
                                 heads(fv, FOX_D), ff + b_fox_f).reshape(b, s, BRANCH_W)

    branches = jnp.stack([ret, gla_o, fox_o], axis=2).astype(h.dtype)
    y_br = jnp.einsum('bsnw,nwd->bsnd', branches, w_br)
    gates = jax.nn.sigmoid(h @ w_mg + b_mg).reshape(b, s, N_BRANCH, D_MODEL)
    mixed = jnp.sum(gates * y_br, axis=2) @ w_o
    x = x + (gate1[:, None, :] * mixed).astype(x.dtype)

    h2 = modulate(rms_norm(x, norm2_g), shift2, scale2)
    u, g = jnp.split(h2 @ w_up, 2, axis=-1)
    u = causal_dwconv(u, w_conv, b_conv)
    y = (jax.nn.silu(u) * g) @ w_down
    x = x + (gate2[:, None, :] * y).astype(x.dtype)
    return x

def first_inputs(seed: int = 0) -> dict:
    key = jax.random.key(seed)
    ks = jax.random.split(key, 24)

    def nrm(k, shape, scale):
        return jax.random.normal(k, shape, F32) * scale

    L, D = DEPTH, D_MODEL
    return {
        'x': nrm(ks[0], (BATCH, SEQ, D), 1.0),
        'c': nrm(ks[1], (BATCH, D), 1.0),
        'norm1_g': 1.0 + nrm(ks[2], (L, D), 0.02),
        'norm2_g': 1.0 + nrm(ks[3], (L, D), 0.02),
        'w_ada': nrm(ks[4], (L, D, 6 * D), 0.5 * D ** -0.5),
        'b_ada': nrm(ks[5], (L, 6 * D), 0.02),
        'w_in': nrm(ks[6], (L, D, IN_W), D ** -0.5),
        'w_gla_a2': nrm(ks[7], (L, GLA_LOWRANK, N_HEADS * GLA_DK), GLA_LOWRANK ** -0.5),
        'b_gla_a': nrm(ks[8], (L, N_HEADS * GLA_DK), 0.1),
        'b_fox_f': 1.0 + nrm(ks[9], (L, N_HEADS), 0.1),
        'ret_norm_g': 1.0 + nrm(ks[10], (L, N_HEADS * RET_DV), 0.02),
        'gla_norm_g': 1.0 + nrm(ks[11], (L, GLA_DV), 0.02),
        'q_norm_g': 1.0 + nrm(ks[12], (L, FOX_D), 0.02),
        'k_norm_g': 1.0 + nrm(ks[13], (L, FOX_D), 0.02),
        'w_br': nrm(ks[14], (L, N_BRANCH, BRANCH_W, D), BRANCH_W ** -0.5),
        'w_mg': nrm(ks[15], (L, D, N_BRANCH * D), D ** -0.5),
        'b_mg': nrm(ks[16], (L, N_BRANCH * D), 0.02),
        'w_o': nrm(ks[17], (L, D, D), D ** -0.5),
        'w_up': nrm(ks[18], (L, D, 2 * D_FF), D ** -0.5),
        'w_conv': nrm(ks[19], (L, CONV_W, D_FF), CONV_W ** -0.5),
        'b_conv': nrm(ks[20], (L, D_FF), 0.02),
        'w_down': nrm(ks[21], (L, D_FF, D), D_FF ** -0.5),
    }

def first_block(x, c, norm1_g, norm2_g, w_ada, b_ada, w_in, w_gla_a2, b_gla_a, b_fox_f,
              ret_norm_g, gla_norm_g, q_norm_g, k_norm_g, w_br, w_mg, b_mg, w_o,
              w_up, w_conv, b_conv, w_down):
    c_act = jax.nn.silu(c)
    for l in range(DEPTH):
        x = hybrid_layer(x, c_act, norm1_g[l], norm2_g[l], w_ada[l], b_ada[l], w_in[l],
                         w_gla_a2[l], b_gla_a[l], b_fox_f[l], ret_norm_g[l], gla_norm_g[l],
                         q_norm_g[l], k_norm_g[l], w_br[l], w_mg[l], b_mg[l], w_o[l],
                         w_up[l], w_conv[l], b_conv[l], w_down[l])
    return x


DEPTH_2 = 4

N_MIXERS = 4
N_A = (DEPTH_2 + 3) // 4
N_B = (DEPTH_2 + 2) // 4
N_C = (DEPTH_2 + 1) // 4
N_D = DEPTH_2 // 4
A_HEADS = 4
A_DV = D_MODEL // A_HEADS
A_DK = A_DV // 2
A_CHUNK = 64
A_IN = 2 * A_HEADS * A_DK + 2 * A_HEADS * A_DV + 2 * A_HEADS
B_HEAD_DIM = 64
B_Q_HEADS = D_MODEL // B_HEAD_DIM
B_KV_HEADS = B_Q_HEADS // 8
B_WINDOW = 128
B_BLOCK = 128
B_IN = (B_Q_HEADS + 2 * B_KV_HEADS) * B_HEAD_DIM
C_EXPAND = 128
C_HEADS = D_MODEL // C_EXPAND
C_DK = C_EXPAND
C_DV = D_MODEL // C_HEADS
C_CHUNK = 16
C_IN = 2 * C_HEADS * C_DK + 2 * C_HEADS * C_DV
D_HEAD_DIM = 64
D_HEADS = D_MODEL // (2 * D_HEAD_DIM)
D_QBLOCK = 128
D_IN = 3 * D_HEADS * 2 * D_HEAD_DIM
ROPE_THETA = 500000.0
ROT_FRAC = 4
FFN_HIDDEN = -(-8 * D_MODEL // (3 * 256)) * 256
DEEPNORM_ALPHA = (2 * DEPTH_2) ** 0.25
DEEPNORM_BETA = (8 * DEPTH_2) ** -0.25
F32_2 = jnp.float32


def layer_norm(x, g, b, eps=1e-5):
    xf = x.astype(F32_2)
    mu = xf.mean(-1, keepdims=True)
    var = jnp.square(xf - mu).mean(-1, keepdims=True)
    return ((xf - mu) * lax.rsqrt(var + eps) * g.astype(F32_2) + b.astype(F32_2)).astype(x.dtype)

def head_rms_norm(h, w, eps=1e-6):
    hf = h.astype(F32_2)
    return hf * lax.rsqrt(jnp.mean(hf * hf, -1, keepdims=True) + eps) * w.astype(F32_2)

def partial_rope(x, positions):
    hd = x.shape[-1]
    rot = hd // ROT_FRAC
    half = rot // 2
    inv = jnp.power(ROPE_THETA, -jnp.arange(half, dtype=F32_2) * 2.0 / rot)
    ang = positions.astype(F32_2)[..., None] * inv
    cos = jnp.cos(ang)[:, :, None, :]
    sin = jnp.sin(ang)[:, :, None, :]
    xf = x.astype(F32_2)
    x1, x2 = xf[..., :half], xf[..., half:rot]
    out = jnp.concatenate([x1 * cos - x2 * sin, x2 * cos + x1 * sin, xf[..., rot:]], axis=-1)
    return out.astype(x.dtype)

def to_chunks(a, L):
    r = a.reshape(a.shape[0], a.shape[1] // L, L, *a.shape[2:])
    return jnp.swapaxes(jnp.moveaxis(r, 1, 0), 2, 3)

def from_chunks(a):
    r = jnp.moveaxis(jnp.swapaxes(a, 2, 3), 0, 1)
    return r.reshape(r.shape[0], r.shape[1] * r.shape[2], *r.shape[3:])

def mlstm_mixer(h, w_in, b_gate, norm_w, w_out):
    bsz, seq, _ = h.shape
    qk, vw = A_HEADS * A_DK, A_HEADS * A_DV
    proj = (h @ w_in).astype(F32_2)
    q = proj[..., :qk].reshape(bsz, seq, A_HEADS, A_DK)
    k = proj[..., qk:2 * qk].reshape(bsz, seq, A_HEADS, A_DK) * (A_DK ** -0.5)
    v = proj[..., 2 * qk:2 * qk + vw].reshape(bsz, seq, A_HEADS, A_DV)
    o = jax.nn.sigmoid(proj[..., 2 * qk + vw:2 * qk + 2 * vw]).reshape(bsz, seq, A_HEADS, A_DV)
    gates = proj[..., 2 * qk + 2 * vw:] + b_gate.astype(F32_2)
    i_pre = gates[..., :A_HEADS]
    log_f = jax.nn.log_sigmoid(gates[..., A_HEADS:])
    causal = jnp.tril(jnp.ones((A_CHUNK, A_CHUNK), bool))

    def step(carry, xs):
        C, n, m = carry
        qc, kc, vc, ic, fc = xs
        b = jnp.cumsum(fc, axis=-1)
        dmat = jnp.where(causal, b[..., :, None] - b[..., None, :] + ic[..., None, :], -jnp.inf)
        m_inter = b + m[..., None]
        m_t = jnp.maximum(m_inter, dmat.max(-1))
        a = jnp.einsum('bhtd,bhsd->bhts', qc, kc) * jnp.exp(dmat - m_t[..., None])
        w_inter = jnp.exp(m_inter - m_t)
        num = jnp.einsum('bhts,bhse->bhte', a, vc) + w_inter[..., None] * jnp.einsum('bhtd,bhde->bhte', qc, C)
        den = a.sum(-1) + w_inter * jnp.einsum('bhtd,bhd->bht', qc, n)
        h_out = num / jnp.maximum(jnp.abs(den), jnp.exp(-m_t))[..., None]
        b_last = b[..., -1]
        g = b_last[..., None] - b + ic
        m_new = jnp.maximum(b_last + m, g.max(-1))
        decay = jnp.exp(b_last + m - m_new)
        ws = jnp.exp(g - m_new[..., None])
        C_new = decay[..., None, None] * C + jnp.einsum('bhs,bhsd,bhse->bhde', ws, kc, vc)
        n_new = decay[..., None] * n + jnp.einsum('bhs,bhsd->bhd', ws, kc)
        return (C_new, n_new, m_new), h_out

    init = (jnp.zeros((bsz, A_HEADS, A_DK, A_DV), F32_2),
            jnp.zeros((bsz, A_HEADS, A_DK), F32_2),
            jnp.zeros((bsz, A_HEADS), F32_2))
    xs = (to_chunks(q, A_CHUNK), to_chunks(k, A_CHUNK), to_chunks(v, A_CHUNK),
          to_chunks(i_pre, A_CHUNK), to_chunks(log_f, A_CHUNK))
    _, ys = lax.scan(step, init, xs)
    hs = from_chunks(ys)
    y = head_rms_norm(hs, norm_w.reshape(A_HEADS, A_DV)) * o
    return y.reshape(bsz, seq, vw).astype(w_out.dtype) @ w_out

def swa_mixer(h, positions, w_in, sinks, w_out):
    bsz, seq, _ = h.shape
    nb = seq // B_BLOCK
    grp = B_Q_HEADS // B_KV_HEADS
    qw, kw = B_Q_HEADS * B_HEAD_DIM, B_KV_HEADS * B_HEAD_DIM
    proj = h @ w_in
    q = partial_rope(proj[..., :qw].reshape(bsz, seq, B_Q_HEADS, B_HEAD_DIM), positions)
    k = partial_rope(proj[..., qw:qw + kw].reshape(bsz, seq, B_KV_HEADS, B_HEAD_DIM), positions)
    v = proj[..., qw + kw:].reshape(bsz, seq, B_KV_HEADS, B_HEAD_DIM)
    qb = jnp.moveaxis(q.reshape(bsz, nb, B_BLOCK, B_KV_HEADS, grp, B_HEAD_DIM), 1, 0)

    def band(a):
        ap = jnp.pad(a, ((0, 0), (B_BLOCK, 0), (0, 0), (0, 0)))
        ap = ap.reshape(bsz, nb + 1, B_BLOCK, B_KV_HEADS, B_HEAD_DIM)
        return jnp.moveaxis(jnp.concatenate([ap[:, :-1], ap[:, 1:]], axis=2), 1, 0)

    kb, vb = band(k), band(v)
    sink = sinks.astype(F32_2).reshape(1, B_KV_HEADS, grp, 1, 1)
    scale = B_HEAD_DIM ** -0.5

    def block(args):
        qi, ki, vi, n = args
        s = jnp.einsum('bqhgd,bkhd->bhgqk', qi, ki, preferred_element_type=F32_2) * scale
        qpos = n * B_BLOCK + jnp.arange(B_BLOCK)
        kpos = (n - 1) * B_BLOCK + jnp.arange(2 * B_BLOCK)
        rel = qpos[:, None] - kpos[None, :]
        valid = (rel >= 0) & (rel < B_WINDOW) & (kpos >= 0)[None, :]
        s = jnp.where(valid, s, -jnp.inf)
        mx = jnp.maximum(s.max(-1, keepdims=True), sink)
        p = jnp.exp(s - mx)
        p = p / (p.sum(-1, keepdims=True) + jnp.exp(sink - mx))
        return jnp.einsum('bhgqk,bkhd->bqhgd', p, vi.astype(F32_2))

    out = lax.map(block, (qb, kb, vb, jnp.arange(nb)))
    out = jnp.moveaxis(out, 0, 1).reshape(bsz, seq, qw)
    return out.astype(w_out.dtype) @ w_out

def hgrn2_mixer(h, lower_bound, w_in, norm_w, w_out):
    bsz, seq, _ = h.shape
    kw, vw = C_HEADS * C_DK, C_HEADS * C_DV
    proj = (h @ w_in).astype(F32_2)
    q = proj[..., :kw]
    f_pre = proj[..., kw:2 * kw]
    i_in = proj[..., 2 * kw:2 * kw + vw]
    g_out = proj[..., 2 * kw + vw:]
    lb = lower_bound.astype(F32_2)
    log_f = jnp.logaddexp(jnp.log(lb), jnp.log1p(-lb) + jax.nn.log_sigmoid(f_pre))
    k = (1.0 - lb) * jax.nn.sigmoid(-f_pre)
    heads = lambda a, d: a.reshape(bsz, seq, C_HEADS, d)
    causal = jnp.tril(jnp.ones((C_CHUNK, C_CHUNK), bool))[:, :, None]

    def step(S, xs):
        qc, kc, vc, fc = xs
        cf = jnp.cumsum(fc, axis=2)
        diff = cf[:, :, :, None, :] - cf[:, :, None, :, :]
        decay = jnp.exp(jnp.where(causal, diff, -jnp.inf))
        a = jnp.einsum('bhtd,bhtsd,bhsd->bhts', qc, decay, kc)
        o = jnp.einsum('bhts,bhse->bhte', a, vc) + jnp.einsum('bhtd,bhde->bhte', qc * jnp.exp(cf), S)
        last = cf[:, :, -1:, :]
        S_new = jnp.exp(last[:, :, 0, :])[..., None] * S + jnp.einsum('bhsd,bhse->bhde', kc * jnp.exp(last - cf), vc)
        return S_new, o

    xs = (to_chunks(heads(q, C_DK), C_CHUNK), to_chunks(heads(k, C_DK), C_CHUNK),
          to_chunks(heads(i_in, C_DV), C_CHUNK), to_chunks(heads(log_f, C_DK), C_CHUNK))
    _, ys = lax.scan(step, jnp.zeros((bsz, C_HEADS, C_DK, C_DV), F32_2), xs)
    o = from_chunks(ys)
    y = head_rms_norm(o, norm_w.reshape(C_HEADS, C_DV)) * jax.nn.silu(heads(g_out, C_DV))
    return y.reshape(bsz, seq, vw).astype(w_out.dtype) @ w_out

def diff_mixer(h, positions, lam_init, w_in, lam_vec, norm_w, w_out):
    bsz, seq, _ = h.shape
    nb = seq // D_QBLOCK
    w = D_HEADS * 2 * D_HEAD_DIM
    proj = h @ w_in
    q = partial_rope(proj[..., :w].reshape(bsz, seq, 2 * D_HEADS, D_HEAD_DIM), positions)
    k = partial_rope(proj[..., w:2 * w].reshape(bsz, seq, 2 * D_HEADS, D_HEAD_DIM), positions)
    q = q.reshape(bsz, seq, D_HEADS, 2, D_HEAD_DIM)
    k = k.reshape(bsz, seq, D_HEADS, 2, D_HEAD_DIM)
    v = proj[..., 2 * w:].reshape(bsz, seq, D_HEADS, 2 * D_HEAD_DIM).astype(F32_2)
    lv = lam_vec.astype(F32_2)
    lam = jnp.exp(jnp.sum(lv[0] * lv[1])) - jnp.exp(jnp.sum(lv[2] * lv[3])) + lam_init
    qb = jnp.moveaxis(q.reshape(bsz, nb, D_QBLOCK, D_HEADS, 2, D_HEAD_DIM), 1, 0)
    kpos = jnp.arange(seq)
    scale = D_HEAD_DIM ** -0.5

    def block(args):
        qi, n = args
        s = jnp.einsum('bqhcd,bkhcd->bhcqk', qi, k, preferred_element_type=F32_2) * scale
        qpos = n * D_QBLOCK + jnp.arange(D_QBLOCK)
        s = jnp.where(kpos[None, :] <= qpos[:, None], s, -jnp.inf)
        p = jax.nn.softmax(s, axis=-1)
        a = p[:, :, 0] - lam * p[:, :, 1]
        return jnp.einsum('bhqk,bkhe->bqhe', a, v)

    out = lax.map(block, (qb, jnp.arange(nb)))
    out = jnp.moveaxis(out, 0, 1).reshape(bsz, seq, D_HEADS, 2 * D_HEAD_DIM)
    out = head_rms_norm(out, norm_w) * (1.0 - lam_init)
    return out.reshape(bsz, seq, w).astype(w_out.dtype) @ w_out

def swiglu(h, w_in, w_out):
    gu = h @ w_in
    return (jax.nn.silu(gu[..., :FFN_HIDDEN]) * gu[..., FFN_HIDDEN:]) @ w_out

def second_inputs(seed: int = 0) -> dict:
    key = jax.random.key(seed)
    ks = jax.random.split(key, 26)
    nrm = lambda k, shape, s: jax.random.normal(k, shape, F32_2) * s
    D = D_MODEL
    beta = DEEPNORM_BETA
    x = nrm(ks[0], (BATCH, SEQ, D), 1.0)
    c = nrm(ks[1], (BATCH, D), 1.0)
    positions = jnp.broadcast_to(jnp.arange(SEQ, dtype=jnp.int32), (BATCH, SEQ))
    ada_w = nrm(ks[2], (DEPTH_2, 2, D, 3 * D), 0.1 * D ** -0.5)
    ada_b = nrm(ks[3], (DEPTH_2, 2, 3 * D), 0.01)
    ln_g = 1.0 + nrm(ks[4], (DEPTH_2, 2, D), 0.02)
    ln_b = nrm(ks[5], (DEPTH_2, 2, D), 0.01)
    mlstm_w_in = nrm(ks[6], (N_A, D, A_IN), D ** -0.5)
    mlstm_b_gate = jnp.concatenate(
        [nrm(ks[7], (N_A, A_HEADS), 0.1),
         jnp.linspace(3.0, 6.0, A_HEADS, dtype=F32_2) + nrm(ks[8], (N_A, A_HEADS), 0.1)], axis=-1)
    mlstm_norm = 1.0 + nrm(ks[9], (N_A, A_HEADS * A_DV), 0.02)
    mlstm_w_out = nrm(ks[10], (N_A, A_HEADS * A_DV, D), beta * (A_HEADS * A_DV) ** -0.5)
    swa_w_in = nrm(ks[11], (N_B, D, B_IN), D ** -0.5)
    swa_sinks = nrm(ks[12], (N_B, B_Q_HEADS), 0.5)
    swa_w_out = nrm(ks[13], (N_B, B_Q_HEADS * B_HEAD_DIM, D), beta * (B_Q_HEADS * B_HEAD_DIM) ** -0.5)
    hgrn_w_in = nrm(ks[14], (N_C, D, C_IN), D ** -0.5)
    hgrn_lower_bounds = nrm(ks[15], (DEPTH_2, C_HEADS * C_DK), 0.1)
    hgrn_norm = 1.0 + nrm(ks[16], (N_C, C_HEADS * C_DV), 0.02)
    hgrn_w_out = nrm(ks[17], (N_C, C_HEADS * C_DV, D), beta * (C_HEADS * C_DV) ** -0.5)
    diff_w_in = nrm(ks[18], (N_D, D, D_IN), D ** -0.5)
    diff_lambda = nrm(ks[19], (N_D, 4, D_HEAD_DIM), 0.1)
    diff_norm = 1.0 + nrm(ks[20], (N_D, 2 * D_HEAD_DIM), 0.02)
    diff_w_out = nrm(ks[21], (N_D, D_HEADS * 2 * D_HEAD_DIM, D), beta * (D_HEADS * 2 * D_HEAD_DIM) ** -0.5)
    ffn_w_in = nrm(ks[22], (DEPTH_2, D, 2 * FFN_HIDDEN), D ** -0.5)
    ffn_w_out = nrm(ks[23], (DEPTH_2, FFN_HIDDEN, D), beta * FFN_HIDDEN ** -0.5)
    return {"x": x, "c": c, "positions": positions, "ada_w": ada_w, "ada_b": ada_b,
            "ln_g": ln_g, "ln_b": ln_b,
            "mlstm_w_in": mlstm_w_in, "mlstm_b_gate": mlstm_b_gate, "mlstm_norm": mlstm_norm,
            "mlstm_w_out": mlstm_w_out,
            "swa_w_in": swa_w_in, "swa_sinks": swa_sinks, "swa_w_out": swa_w_out,
            "hgrn_w_in": hgrn_w_in, "hgrn_lower_bounds": hgrn_lower_bounds, "hgrn_norm": hgrn_norm,
            "hgrn_w_out": hgrn_w_out,
            "diff_w_in": diff_w_in, "diff_lambda": diff_lambda, "diff_norm": diff_norm,
            "diff_w_out": diff_w_out,
            "ffn_w_in": ffn_w_in, "ffn_w_out": ffn_w_out}

def second_block(x, c, positions, ada_w, ada_b, ln_g, ln_b,
              mlstm_w_in, mlstm_b_gate, mlstm_norm, mlstm_w_out,
              swa_w_in, swa_sinks, swa_w_out,
              hgrn_w_in, hgrn_lower_bounds, hgrn_norm, hgrn_w_out,
              diff_w_in, diff_lambda, diff_norm, diff_w_out,
              ffn_w_in, ffn_w_out):
    cond = jax.nn.silu(c.astype(F32_2))
    lbs = jnp.cumsum(jax.nn.softmax(hgrn_lower_bounds.astype(F32_2), axis=0), axis=0)
    lbs = lbs - lbs[0]
    for i in range(DEPTH_2):
        mixer, j = i % N_MIXERS, i // N_MIXERS
        mod = jnp.einsum('bd,sde->sbe', cond, ada_w[i].astype(F32_2)) + ada_b[i][:, None, :].astype(F32_2)
        shift, scale, gate = jnp.split(mod.astype(x.dtype), 3, axis=-1)
        h = x * (1 + scale[0][:, None]) + shift[0][:, None]
        if mixer == 0:
            y = mlstm_mixer(h, mlstm_w_in[j], mlstm_b_gate[j], mlstm_norm[j], mlstm_w_out[j])
        elif mixer == 1:
            y = swa_mixer(h, positions, swa_w_in[j], swa_sinks[j], swa_w_out[j])
        elif mixer == 2:
            y = hgrn2_mixer(h, lbs[i], hgrn_w_in[j], hgrn_norm[j], hgrn_w_out[j])
        else:
            lam_init = 0.8 - 0.6 * math.exp(-0.3 * i)
            y = diff_mixer(h, positions, lam_init, diff_w_in[j], diff_lambda[j], diff_norm[j], diff_w_out[j])
        x = layer_norm(DEEPNORM_ALPHA * x + (1 + gate[0][:, None]) * y.astype(x.dtype), ln_g[i, 0], ln_b[i, 0])
        h = x * (1 + scale[1][:, None]) + shift[1][:, None]
        y = swiglu(h, ffn_w_in[i], ffn_w_out[i])
        x = layer_norm(DEEPNORM_ALPHA * x + (1 + gate[1][:, None]) * y.astype(x.dtype), ln_g[i, 1], ln_b[i, 1])
    return x


def setup_inputs(seed=0):
    out = dict(first_inputs(seed))
    for name, value in second_inputs(seed + 1).items():
        if name != "x":
            out[name + "_2"] = value
    return out


def reference(
    x, c, norm1_g, norm2_g, w_ada, b_ada, w_in, w_gla_a2, b_gla_a, b_fox_f, ret_norm_g,
    gla_norm_g, q_norm_g, k_norm_g, w_br, w_mg, b_mg, w_o, w_up, w_conv, b_conv, w_down, c_2,
    positions_2, ada_w_2, ada_b_2, ln_g_2, ln_b_2, mlstm_w_in_2, mlstm_b_gate_2, mlstm_norm_2,
    mlstm_w_out_2, swa_w_in_2, swa_sinks_2, swa_w_out_2, hgrn_w_in_2, hgrn_lower_bounds_2,
    hgrn_norm_2, hgrn_w_out_2, diff_w_in_2, diff_lambda_2, diff_norm_2, diff_w_out_2,
    ffn_w_in_2, ffn_w_out_2,
):
    x = first_block(
        x, c, norm1_g, norm2_g, w_ada, b_ada, w_in, w_gla_a2, b_gla_a, b_fox_f, ret_norm_g,
        gla_norm_g, q_norm_g, k_norm_g, w_br, w_mg, b_mg, w_o, w_up, w_conv, b_conv, w_down,
    )
    return second_block(
        x, c_2, positions_2, ada_w_2, ada_b_2, ln_g_2, ln_b_2, mlstm_w_in_2, mlstm_b_gate_2,
        mlstm_norm_2, mlstm_w_out_2, swa_w_in_2, swa_sinks_2, swa_w_out_2, hgrn_w_in_2,
        hgrn_lower_bounds_2, hgrn_norm_2, hgrn_w_out_2, diff_w_in_2, diff_lambda_2, diff_norm_2,
        diff_w_out_2, ffn_w_in_2, ffn_w_out_2,
    )


_drawn_inputs = setup_inputs


def setup_inputs(seed=0):
    import zlib

    import numpy as np

    out = dict(_drawn_inputs(seed))
    spreads = {}
    factors = {'norm1_g': 5.105,
     'norm2_g': 5.948,
     'b_gla_a': 6.857,
     'b_fox_f': 7.097,
     'ret_norm_g': 8.0,
     'gla_norm_g': 8.0,
     'q_norm_g': 8.0,
     'k_norm_g': 8.0,
     'b_mg': 8.0,
     'b_conv': 8.0,
     'ada_b_2': 5.1,
     'mlstm_norm_2': 64.0,
     'swa_sinks_2': 8.0,
     'hgrn_lower_bounds_2': 5.799,
     'hgrn_norm_2': 8.0,
     'diff_norm_2': 87.958}
    for name, (base, spread) in spreads.items():
        noise = np.random.default_rng([zlib.crc32(name.encode()), seed]).standard_normal(out[name].shape)
        drawn = base * np.exp(spread * noise) if base else spread * noise
        out[name] = jnp.asarray(drawn.astype(out[name].dtype))
    for name, factor in factors.items():
        out[name] = (out[name] * factor).astype(out[name].dtype)
    return out
```

```python
from contextlib import ExitStack
import math

import numpy as np
import concourse.bass as bass
import concourse.mybir as mybir

F32 = mybir.dt.float32
F32R = mybir.dt.float32r
I32 = mybir.dt.int32
ALU = mybir.AluOpType
ACT = mybir.ActivationFunctionType
AX = mybir.AxisListType.X

P = 128
D = 1024
S = 256
KT = D // P
TT = S // P
F_HID = 2816
PC = 256
PIECE = KT * PC
N_UP = F_HID // PC
N_ADA1 = 6 * D // PC
N_ADA2 = 3 * D // PC
HEADS = 4
NEG = -float(2 ** 100)
ALPHA = 8 ** 0.25
TWO_PI = 2 * math.pi

COLS = {}


def _columns():
    at = 0
    for name, tiles in (
            [(f"{n}{l}", k) for l in range(2) for n, k in (
                ("norm1_g", 8), ("norm2_g", 8), ("b_ada", 48), ("ret_norm_g", 4), ("gla_norm_g", 1),
                ("q_norm_g", 1), ("k_norm_g", 1), ("b_mg", 24), ("w_conv", 66), ("b_conv", 22), ("b_fox_f", 1))]
            + [(f"ada_b_2{i}", 48) for i in range(4)] + [(f"ln_g_2{i}", 16) for i in range(4)]
            + [(f"ln_b_2{i}", 16) for i in range(4)]
            + [("mlstm_norm", 8), ("b_gate", 1), ("hgrn_lb", 32), ("hgrn_norm", 8), ("diff_norm", 1)]):
        COLS[name] = (at, tiles)
        at += tiles
    return at


N_COLS = _columns()


def constants():
    i = np.arange(P)
    u, t = i[:, None], i[None, :]
    f = np.float32
    always = {
        "ident": np.eye(P, dtype=f),
        "mean_d": np.full((P, P), 1 / D, f),
        "mean_h": np.full((P, P), 1 / P, f),
        "ones": np.ones((P, P), f),
        "tri": np.concatenate([(u + P * k <= np.arange(S)[None, :]).astype(f) for k in range(TT)], 1),
        "mask_after": np.where(t > u, f(NEG), f(0)).astype(f),
        "mask_band": np.where(t <= u, f(NEG), f(0)).astype(f),
        "gla_suffix": ((u > t) & (u // 64 == t // 64)).astype(f) / 16,
        "gla_chunk": np.stack([(i < 64), (i >= 64)], 1).astype(f) / 16,
    }
    pick = np.zeros((P, HEADS, S), f)
    for h in range(HEADS):
        pick[h, h] = 1
    always["pick"] = pick.reshape(P, -1)
    always["unpick"] = -pick[:, :, :P].reshape(P, -1)

    def swap(group, half):
        m = np.zeros((P, P), f)
        for o in range(P):
            r = o % group
            if r < half:
                m[o + half, o] = -1
            elif r < 2 * half:
                m[o - half, o] = 1
        return m

    always["swap16"] = swap(64, 8)
    inv = np.zeros((P, 1), f)
    for p in range(P):
        if p % 64 < 16:
            inv[p] = np.power(f(500000.0), -f(p % 8) * f(2.0) / f(16))
    always["inv16"] = inv

    first = {"swap128": swap(128, 64)}
    inv = (f(10000.0) ** (-np.arange(64, dtype=f) / f(64))).astype(f)
    ang = np.concatenate([inv, inv])[:, None] * np.arange(S, dtype=f)[None, :]
    first["cos128"], first["sin128"] = np.cos(ang).astype(f), np.sin(ang).astype(f)
    tab = np.zeros((P, HEADS, 3, P), np.float64)
    for h in range(HEADS):
        lg = np.log1p(-2.0 ** (-5.0 - h))
        j, q = u.astype(float), t.astype(float)
        diag = np.where(j // 64 <= q // 64, np.exp(np.abs(q - j) * lg), 0)
        off = np.exp((q + P - j) * lg)
        tab[:, h] = np.stack([diag, off, diag], 1)
    first["ret_decay"] = (tab * P ** -0.5).reshape(P, -1).astype(f)

    hg = np.zeros((P, 9, P), f)
    mask = np.zeros((P, 8, P), f)
    for n, b in enumerate((1, 2, 4, 8, 16, 32, 64)):
        same = u // b == t // b
        odd = (t // b) % 2 == 1
        hg[:, n] = np.where(odd, same & (u <= t), same & (u > t))
        mask[:, n] = (u // (2 * b) == t // (2 * b)) & ((u // b) % 2 == 0) & odd
    hg[:, 7] = u > t
    hg[:, 8] = u <= t
    mask[:, 7] = u == t
    third = {"hg_decay": hg.reshape(P, -1), "hg_mask": mask.reshape(P, -1)}
    return always, first, third


def _join(parts):
    at, where, cols = 0, {}, []
    for name, a in parts.items():
        where[name] = (at, a.shape[1])
        at += a.shape[1]
        cols.append(a)
    return np.ascontiguousarray(np.concatenate(cols, 1), np.float32), where


class Mark(tuple):
    pass


class Queue:

    def __init__(self, sem):
        self.sem, self.count, self.steps, self.waited = sem, 0, [], {}

    def wait(self, *marks):
        for m in marks:
            if m is None:
                continue
            if not isinstance(m, Mark):
                self.wait(*m)
                continue
            sem, value = m
            if self.waited.get(id(sem), 0) < value:
                self.waited[id(sem)] = value
                self.steps.append((None, sem, value))

    def do(self, make, *marks):
        self.wait(*marks)
        self.count += 1
        self.steps.append((make, self.sem, 1))
        return Mark((self.sem, self.count))

    def last(self):
        return Mark((self.sem, self.count)) if self.count else None

    def emit(self, eng):
        for make, sem, value in self.steps:
            if make is None:
                eng.wait_ge(sem, value)
            elif sem is None:
                make(eng)
            else:
                make(eng).then_inc(sem, value)


class TensorQueue(Queue):
    def mm(self, out, lhsT, rhs, start=True, stop=True, free=False):
        self.steps.append((lambda e: e.matmul(out, lhsT, rhs, start=start, stop=stop, skip_group_check=free), None, 0))

    def turn(self, out, in_, ident):
        self.steps.append((lambda e: e.transpose(out, in_, ident), None, 0))

    def mark(self):
        make, sem, _ = self.steps[-1]
        assert make is not None and sem is None
        self.count += 1
        self.steps[-1] = (make, self.sem, 1)
        return Mark((self.sem, self.count))


class Slot:

    def __init__(self, ap):
        self.ap, self.free = ap, []


class Ring:
    def __init__(self, aps):
        self.slots, self.n = [Slot(a) for a in aps], 0

    def next(self):
        s = self.slots[self.n % len(self.slots)]
        self.n += 1
        return s


class Split:

    def __init__(self, hi, lo, tiles):
        self.hi, self.lo, self.marks = hi, lo, [None] * tiles


def build(nc, a, plan, const_at):
    wanted = []
    where0, where1, where3 = const_at
    ctx = ExitStack()
    with ctx:
        def sb(name, cols, dt=F32, parts=P):
            return ctx.enter_context(nc.sbuf_tensor(name, [parts, cols], dt))[:, :]

        def sem(name):
            return ctx.enter_context(nc.semaphore(name))

        RAW, PARTS, AHEAD = 5, 2, 2
        raw_ring = [sb(f"raw{i}", PIECE) for i in range(RAW)]
        hi_ring = [sb(f"w_hi{i}", PIECE, F32R) for i in range(PARTS)]
        lo_ring = [sb(f"w_lo{i}", PIECE, F32R) for i in range(PARTS)]
        x = sb("x", KT * S).rearrange("p (t n) -> p t n", t=KT)
        t1 = sb("t1", KT * S).rearrange("p (t n) -> p t n", t=KT)
        h_hi = sb("h_hi", KT * S, F32R).rearrange("p (t n) -> p t n", t=KT)
        h_lo = sb("h_lo", KT * S, F32R).rearrange("p (t n) -> p t n", t=KT)
        b_hi = sb("b_hi", 3 * HEADS * S, F32R)
        b_lo = sb("b_lo", 3 * HEADS * S, F32R)
        c0 = sb("const_always", a["const0"].shape[1])
        c1 = sb("const_phase", max(a["const1"].shape[1], a["const3"].shape[1]))
        cols = sb("cols", N_COLS)
        mod = sb("mod", 2 * 48 + 4 * 48)
        small = sb("small", 128)
        rope16 = sb("rope16", 2 * S).rearrange("p (k n) -> p k n", k=2)
        ARENA = 10760
        arena = sb("arena", ARENA)

        banks_a = ctx.enter_context(nc.psum_tensor("banks_a", [P, 4, 512], F32))
        banks_b = ctx.enter_context(nc.psum_tensor("banks_b", [P, 3, 512], F32))
        scratch = Ring([banks_a[:, i, :] for i in range(4)])
        proj = Ring([banks_b[:, i, :] for i in range(3)])

        T, V, A, G = TensorQueue(sem("s_tensor")), Queue(sem("s_vector")), Queue(sem("s_scalar")), Queue(sem("s_gpsimd"))
        L = Queue(None)
        raw_sem = [sem(f"s_raw{i}") for i in range(RAW)]
        s_in = {n: sem(f"s_in_{n}") for n in ("x", "c_rows", "c_rows2", "const0", "const1", "const3", "cols", "wa20", "wa21", "sinks", "lam", "pos")}
        s_out = sem("s_out")

        def load(dst, name, *marks):
            L.wait(*marks)
            L.steps.append((lambda e: e.dma_start(dst, a[name]), s_in[name], 16))
            return Mark((s_in[name], 16))

        def con(name):
            for base, where in ((c0, where0),):
                if name in where:
                    at, n = where[name]
                    return base[:, at:at + n]
            at, n = (where1 if name in where1 else where3)[name]
            return c1[:, at:at + n]

        def col(name, t=0, n=1):
            return cols[:, COLS[name][0] + t:COLS[name][0] + t + n]

        table = [None]

        def v_tt(out, x0, x1, op, *m):
            return V.do(lambda e: e.tensor_tensor(out, x0, x1, op), *m)

        def v_ts(out, x0, s1, s2, op0, op1, *m):
            if op1 is None:
                return V.do(lambda e: e.tensor_scalar(out, x0, s1, None, op0), *m)
            return V.do(lambda e: e.tensor_scalar(out, x0, s1, s2, op0, op1), *m)

        def v_stt(out, x0, s, x1, op0, op1, *m):
            return V.do(lambda e: e.scalar_tensor_tensor(out=out, in0=x0, scalar=s, in1=x1, op0=op0, op1=op1), *m)

        def v_copy(out, x0, *m):
            return V.do(lambda e: e.tensor_copy(out, x0), *m)

        def v_recip(out, x0, *m):
            return V.do(lambda e: e.reciprocal(out, x0), *m)

        def preload_exp():
            if table[0] != "exp":
                A.steps.append((lambda e: e.preload_act_table_set("natural_log_exp_and_others"), None, 0))
                table[0] = "exp"

        def preload_silu():
            A.steps.append((lambda e: e.preload_act_table_set("silu_and_others"), None, 0))
            table[0] = None

        def a_act(out, x0, func, *m, bias=0.0, scale=1.0, accum=None):
            if func in (ACT.Exp, ACT.Ln):
                preload_exp()
            elif func in (ACT.Silu, ACT.Sigmoid, ACT.Sin):
                table[0] = None
            if accum is not None:
                return A.do(lambda e: e.activation(out, x0, func, bias=bias, scale=scale, accum_out=accum), *m)
            return A.do(lambda e: e.activation(out, x0, func, bias=bias, scale=scale), *m)

        def a_copy(out, x0, *m, scale=1.0):
            return A.do(lambda e: e.activation(out, x0, ACT.Copy, scale=scale), *m)

        def g_tt(out, x0, x1, op, *m):
            return G.do(lambda e: e.tensor_tensor(out, x0, x1, op), *m)

        def g_sub(out, x0, x1, *m):
            return G.do(lambda e: e.tensor_tensor(out, x0, x1, ALU.subtract), *m)

        def g_ts(out, x0, s1, s2, *m):
            return G.do(lambda e: e.tensor_scalar(out, x0, s1, s2, ALU.mult, ALU.add), *m)

        def flat(ap):
            return ap.rearrange("p t n -> p (t n)")

        class Piece:
            pass

        raws = [Slot(r) for r in raw_ring]
        parts = [Slot((h, l)) for h, l in zip(hi_ring, lo_ring)]
        st = {"taken": 0, "loaded": 0, "split": 0, "parted": 0, "ahead": 0}
        pieces = []

        def pump(sub=None):
            moved = True
            while moved:
                moved = False
                n = st["loaded"]
                if n < len(plan) and (n < RAW or pieces[n - RAW].raw_free is not None):
                    name, idx, width, split = plan[n]
                    p = Piece()
                    p.raw, p.width, p.split = raw_ring[n % RAW][:, 0:width], width, split
                    p.raw_free, p.hi = None, None
                    if n >= RAW:
                        L.wait(*pieces[n - RAW].raw_free)
                    src = a[name][idx]
                    L.steps.append((lambda e, p=p, src=src: e.dma_start(p.raw, src), raw_sem[n % RAW], 16))
                    p.loaded = Mark((raw_sem[n % RAW], 16 * (n // RAW + 1)))
                    pieces.append(p)
                    st["loaded"] += 1
                    moved = True
                n = st["split"]
                if n < st["loaded"] and n <= st["taken"] + st["ahead"]:
                    p = pieces[n]
                    if not p.split:
                        st["split"] += 1
                        moved = True
                    elif parts[st["parted"] % PARTS].free is not None:
                        slot = parts[st["parted"] % PARTS]
                        hi, lo = slot.ap[0][:, 0:p.width], slot.ap[1][:, 0:p.width]
                        p.hi, p.lo, p.slot, p.parted = hi, lo, slot, []
                        for c in (slice(0, p.width // 2), slice(p.width // 2, p.width)):
                            m_hi = a_copy(hi[:, c], p.raw[:, c], p.loaded, slot.free)
                            m_lo = (sub or v_tt)(lo[:, c], p.raw[:, c], hi[:, c].bitcast(F32), ALU.subtract, p.loaded, m_hi, slot.free)
                            p.parted.append((m_hi, m_lo))
                        slot.free = None
                        p.raw_free = [m_hi, m_lo]
                        st["parted"] += 1
                        st["split"] += 1
                        moved = True

        def take(name, idx, width=PIECE, split=True, hold=False):
            wanted.append((name, idx, width, split))
            if plan is None:
                p = Piece()
                p.raw, p.hi, p.lo = raw_ring[0][:, 0:width], hi_ring[0][:, 0:width], lo_ring[0][:, 0:width]
                p.parted, p.loaded, p.slot = [None, None], None, Slot(None)
                p.split = split
                return p
            if not hold or st["split"] <= st["taken"]:
                pump()
            p = pieces[st["taken"]]
            assert plan[st["taken"]] == (name, idx, width, split)
            st["taken"] += 1
            return p

        def give_back(p, mark):
            if p.split:
                p.slot.free = [mark]
            else:
                p.raw_free = [mark]

        def gemm_fm(p, act, bank, n_tiles=PC // P, kts=KT, width=PC, k0=0):
            T.wait(bank.free)
            hi = p.hi.rearrange("p (k n) -> p k n", k=kts)
            lo = p.lo.rearrange("p (k n) -> p k n", k=kts)
            for n in range(n_tiles):
                out = bank.ap[:, n * S:(n + 1) * S]
                c = slice(n * P, (n + 1) * P)
                for k in range(kts):
                    T.wait(p.parted[2 * k // kts], act.marks[k0 + k])
                    ah, al = act.hi[:, k0 + k, :], act.lo[:, k0 + k, :]
                    T.mm(out, hi[:, k, c], ah, start=(k == 0), stop=False)
                    T.mm(out, hi[:, k, c], al, start=False, stop=False)
                    T.mm(out, lo[:, k, c], ah, start=False, stop=(k == kts - 1))
            m = T.mark()
            give_back(p, m)
            return m

        def gemm_tm(p, act, bank):
            T.wait(bank.free)
            hi = p.hi.rearrange("p (k n) -> p k n", k=KT)
            lo = p.lo.rearrange("p (k n) -> p k n", k=KT)
            for t in range(TT):
                out = bank.ap[:, t * PC:(t + 1) * PC]
                r = slice(t * P, (t + 1) * P)
                for k in range(KT):
                    T.wait(p.parted[2 * k // KT], act.marks[k])
                    T.mm(out, act.hi[:, k, r], hi[:, k, :], start=(k == 0), stop=False)
                    T.mm(out, act.hi[:, k, r], lo[:, k, :], start=False, stop=False)
                    T.mm(out, act.lo[:, k, r], hi[:, k, :], start=False, stop=(k == KT - 1))
            m = T.mark()
            give_back(p, m)
            return m

        def pace(steps=1):
            done["pieces"] += steps
            while ada["n"] < len(todo) and ada["n"] < ADA_AHEAD + ADA_RATE * done["pieces"]:
                ada_step()

        def project(name, idx, act, tm=False, last=False):
            if not last:
                pace()
            p = take(name, idx, hold=last)
            bank = proj.next()
            m = (gemm_tm if tm else gemm_fm)(p, act, bank)
            return bank, m

        def split_ahead():
            if plan is not None:
                pump(g_tt)

        def split_into(hi, lo, src, *marks, on_pool=True):
            m_hi = a_copy(hi, src, *marks)
            sub = g_sub if on_pool else (lambda o, p0, p1, *m: v_tt(o, p0, p1, ALU.subtract, *m))
            m_lo = sub(lo, src, hi.bitcast(F32), m_hi, *marks)
            return (m_hi, m_lo)

        MOD = [0, 48, 96, 144, 192, 240]
        bias_of = [("b_ada0", 0), ("b_ada1", 0)] + [(f"ada_b_2{i}", 0) for i in range(4)]
        mod_mark = [None] * 6
        todo = [(l, n) for l in range(2) for n in range(N_ADA1)] + [(2 + i, n) for i in range(4) for n in range(2 * N_ADA2)]
        ada = {"n": 0}
        done = {"pieces": 0}
        ADA_AHEAD, ADA_RATE, PACE_ITEM, PACE_HEAD = 7, 0.5, 0, 0
        c_rows = sb("c_rows", D)
        c_of = {}

        def load_c(name, *marks):
            m = load(c_rows, name, *marks)
            c_of["mark"] = a_act(c_rows, c_rows, ACT.Silu, m)

        def ada_step():
            g, n = todo[ada["n"]]
            ada["n"] += 1
            if g == 2 and n == 0:
                load_c("c_rows2", mod_mark[1])
            p = take("w_ada" if g < 2 else "ada_w_2", (g if g < 2 else g - 2, n), split=False)
            out = mod[:, MOD[g] + 2 * n:MOD[g] + 2 * n + 2]
            for j in range(2):
                w = p.raw[:, j * D:(j + 1) * D]
                m = V.do(lambda e, w=w, j=j: e.tensor_tensor_reduce(w, w, c_rows, 1.0, 0.0, ALU.mult, ALU.add, out[:, j:j + 1]),
                         p.loaded, c_of["mark"])
            give_back(p, m)
            b = COLS[bias_of[g][0]][0] + 2 * n
            mod_mark[g] = v_tt(out, out, cols[:, b:b + 2], ALU.add, m, m_cols)

        def ada_until(g, n=None):
            end = (g, 24 if n is None else n)
            while ada["n"] < len(todo) and todo[ada["n"]] < end:
                ada_step()

        def everyone():
            return [q.last() for q in (T, V, A, G)]

        def new_phase(ends=None):
            ends = ends or everyone()
            for q in (T, V, A, G):
                q.wait(*ends)

        x_ready = [None] * KT
        load_c("c_rows")
        m_cols = load(cols, "cols")
        m_x = load(flat(x), "x")
        m_c0 = load(c0, "const0")
        if plan is not None:
            pump()
        ident, ones = con("ident"), con("ones")
        x_ready[:] = [m_x] * KT
        T.wait(m_c0)
        V.wait(m_c0, m_cols)
        A.wait(m_cols)

        def rstd(out, bank_ap, eps, *marks, scale=1.0):
            m = a_act(out, bank_ap, ACT.Ln, *marks, bias=eps, scale=scale)
            return m, a_act(out, out, ACT.Exp, m, scale=-0.5)

        rope_buf = sb("rope_tmp", 1024)
        rope_tmp = Ring([rope_buf[:, i * 512:(i + 1) * 512].rearrange("p (t n) -> p t n", t=2) for i in range(2)])
        diag = Slot(sb("diag", S))
        tok = sb("token_stats", 16)
        pair_sum = Slot(sb("pair_sum", S))
        gains = sb("norm_gains", 40)
        gate_sb, gain_sb, shift_sb, x_gain, x_shift = (gains[:, 8 * k:8 * k + 8] for k in range(5))

        def column_sums(bank, at, tile, first, *marks):
            T.wait(marks)
            for t in range(TT):
                T.mm(bank.ap[:, at + t:at + t + 1], tile[:, t * P:(t + 1) * P], con("mean_d")[:, 0:1],
                     start=(first and t == 0), stop=False, free=True)

        def add_halves(s, m, on_vector):
            add = v_tt if on_vector else g_tt
            return add(s.ap[:, 0, :], s.ap[:, 0, :], s.ap[:, 1, :], ALU.add, m)

        def to_diagonals(src, m):
            for t in range(TT):
                md = v_ts(diag.ap[:, t * P:(t + 1) * P], ident, src[:, t:t + 1], None, ALU.mult, None, m, diag.free)
            return md

        def on_every_partition(bank, m, *marks):
            T.wait(m, *marks)
            for t in range(TT):
                T.mm(bank.ap[:, t * P:(t + 1) * P], ones, diag.ap[:, t * P:(t + 1) * P])
            m = T.mark()
            diag.free = [m]
            return m

        def inverse_root(v, m):
            y, z = tok[:, 8:10], tok[:, 10:12]
            m = a_act(y, v, ACT.Ln, m)
            m = a_act(y, y, ACT.Exp, m, scale=-0.5)

            def newton():
                m1 = v_stt(z, y, -0.5, y, ALU.mult, ALU.mult, m)
                m1 = v_tt(z, z, v, ALU.mult, m1)
                return y, v_stt(y, z, 1.5, y, ALU.add, ALU.mult, m1)
            return newton

        h = Split(h_hi, h_lo, KT)

        def split_h(t, src, m, m_free):
            h.marks[t] = split_into(h.hi[:, t, :], h.lo[:, t, :], src, m, m_free)

        class Update:

            def __init__(self, ring, gate):
                self.ring, self.gate = ring, gate

            def finish(self, t, y, m):
                x_ready[t] = v_stt(x[:, t, :], y, self.gate[:, t:t + 1], x[:, t, :], ALU.mult, ALU.add, m, x_ready[t], self.m_gain)
                if t % 2:
                    self.after_pair(t // 2)
                return x_ready[t]

            def after_pair(self, k):
                pass

        def pair(ap, k):
            return flat(ap[:, 2 * k:2 * k + 2, :])

        class ToRms(Update):

            def __init__(self, ring, gate, norm, g, part, gate_mark=None):
                super().__init__(ring, gate)
                self.norm, self.g, self.at = norm, g, MOD[g] + 24 * part
                self.part, self.m_gain = part, gate_mark

            def columns(self):
                self.m_col = v_stt(gain_sb, mod[:, self.at + 8:self.at + 16], 1.0, col(*self.norm, 8), ALU.add, ALU.mult,
                                   mod_mark[self.g], V.last(), x_ready)

            def square(self, k):
                s = rope_tmp.next()
                m = a_act(flat(s.ap), pair(x, k), ACT.Square, x_ready[2 * k:2 * k + 2], s.free)
                self.squared[k] = s, add_halves(s, m, k == KT // 2 - 1)

            def sum_squares(self, k):
                if k == 0:
                    self.bank = self.ring.next()
                    T.wait(self.bank.free)
                s, m = self.squared[k]
                column_sums(self.bank, 0, s.ap[:, 0, :], k == 0, m)
                m = T.mark()
                s.free = [m]
                return m

            def before(self, k):
                if k == 0:
                    self.squared = {}
                if k >= 2:
                    self.sum_squares(k - 2)
                if k:
                    self.square(k - 1)

            def root(self):
                preload_exp()
                self.sum_squares(KT // 2 - 2)
                self.square(KT // 2 - 1)
                if self.gate is not None:
                    split_ahead()
                m = self.sum_squares(KT // 2 - 1)
                v = tok[:, 0:2]
                m = v_ts(v, self.bank.ap[:, 0:2], 1e-6, None, ALU.add, None, m)
                self.bank.free = [m]
                y, m = inverse_root(v, m)()
                md = to_diagonals(y, m)
                b = self.ring.next()
                return b, on_every_partition(b, md, b.free)

            def end(self, root=None):
                ends = everyone()
                b, mr = root or self.root()
                for k in range(KT // 2):
                    s = rope_tmp.next()
                    for j in range(2):
                        t = 2 * k + j
                        m = v_tt(s.ap[:, j, :], x[:, t, :], b.ap[:, 0:S], ALU.mult, mr, x_ready[t], s.free)
                        m = v_ts(s.ap[:, j, :], s.ap[:, j, :], gain_sb[:, t:t + 1], mod[:, self.at + t:self.at + t + 1],
                                 ALU.mult, ALU.add, m, self.m_col)
                        split_h(t, s.ap[:, j, :], m, ends)
                    s.free = [h.marks[2 * k], h.marks[2 * k + 1]]
                b.free = [V.last()]
                new_phase(ends)

        class ToPlain(Update):

            def __init__(self, ring, gate, g, gate_mark):
                super().__init__(ring, gate)
                self.g, self.m_gain = g, gate_mark

            def columns(self):
                self.m_col = v_ts(gain_sb, mod[:, MOD[self.g] + 8:MOD[self.g] + 16], 1.0, None, ALU.add, None, mod_mark[self.g], V.last(), x_ready)

            def input_pair(self, k, ends):
                s = rope_tmp.next()
                at = MOD[self.g]
                for j in range(2):
                    t = 2 * k + j
                    m = v_ts(s.ap[:, j, :], x[:, t, :], gain_sb[:, t:t + 1], mod[:, at + t:at + t + 1],
                             ALU.mult, ALU.add, self.m_col, x_ready[t], s.free)
                    split_h(t, s.ap[:, j, :], m, ends)
                s.free = [h.marks[2 * k], h.marks[2 * k + 1]]
                m = a_act(pair(x, k), pair(x, k), ACT.Copy, m, scale=ALPHA)
                x_ready[2 * k] = x_ready[2 * k + 1] = m

            def before(self, k):
                if k == 0:
                    self.ends = everyone()
                elif k:
                    self.input_pair(k - 1, self.ends)

            def end(self):
                ends = everyone()
                self.input_pair(KT // 2 - 1, ends)
                new_phase(ends)

        class ToLayerNorm(Update):

            def __init__(self, ring, i, s, g, nxt):
                super().__init__(ring, gate_sb)
                self.g, self.gate_at, self.nxt = g, MOD[g] + 24 * s + 16, nxt
                self.ln_g, self.ln_b = col(f"ln_g_2{i}", 8 * s, 8), col(f"ln_b_2{i}", 8 * s, 8)

            def columns(self):
                last = V.last()
                self.m_gain = v_ts(gate_sb, mod[:, self.gate_at:self.gate_at + 8], 1.0, None, ALU.add, None, mod_mark[self.g], last, x_ready)
                if self.nxt is None:
                    return
                g, part = self.nxt
                at = MOD[g] + 24 * part
                shift, scale = mod[:, at:at + 8], mod[:, at + 8:at + 16]
                m1 = v_stt(gain_sb, scale, 1.0, self.ln_g, ALU.add, ALU.mult, mod_mark[g], last, h.marks)
                m2 = v_stt(shift_sb, scale, 1.0, self.ln_b, ALU.add, ALU.mult, mod_mark[g], last, h.marks)
                m2 = v_tt(shift_sb, shift_sb, shift, ALU.add, m2)
                m3 = v_ts(x_gain, self.ln_g, ALPHA, None, ALU.mult, None, last)
                m4 = v_ts(x_shift, self.ln_b, ALPHA, None, ALU.mult, None, last)
                self.m_col = [m1, m2, m3, m4]

            def sums(self, k):
                if k == 0:
                    self.bank, self.wide, self.wide2 = (self.ring.next() for _ in range(3))
                    T.wait(self.bank.free)
                    self.read = None
                column_sums(self.bank, 0, pair_sum.ap, k == 0, self.m_pair, self.read)
                m = T.mark()
                pair_sum.free = [m]
                return m

            def after_pair(self, k):
                add = g_tt if k in (1, 2) else v_tt
                self.m_pair = add(pair_sum.ap, x[:, 2 * k, :], x[:, 2 * k + 1, :], ALU.add, x_ready[2 * k:2 * k + 2], pair_sum.free)

            def center(self, k):
                for t in (2 * k, 2 * k + 1):
                    m = v_tt(t1[:, t, :], x[:, t, :], self.wide.ap[:, 0:S], ALU.subtract, self.m_c, x_ready[t])
                s = rope_tmp.next()
                m_sq = a_act(flat(s.ap), pair(t1, k), ACT.Square, m, s.free)
                return s, add_halves(s, m_sq, k == KT // 2 - 1), m_sq

            def square_sums(self, s, m, m_sq):
                column_sums(self.bank, 2, s.ap[:, 0, :], False, m, self.read)
                m = T.mark()
                s.free = [m]
                return m

            def before(self, k):
                c = tok[:, 0:2]
                if k == 1:
                    m = self.sums(0)
                    self.read = m = v_ts(c, self.bank.ap[:, 0:2], 4.0, None, ALU.mult, None, m, V.last())
                    self.m_cd = m
                    self.m_diag = to_diagonals(c, m)
                if k == 2:
                    self.m_c = on_every_partition(self.wide, self.m_diag, self.wide.free)
                    self.sums(1)
                    self.sq = [self.center(0), self.center(1)]
                if k == 3:
                    self.sums(2)
                    for z in self.sq:
                        self.square_sums(*z)
                    preload_exp()
                    self.sq = [self.center(2)]

            def end(self):
                ends = everyone()
                self.sq.append(self.center(3))
                split_ahead()
                m = self.sums(3)
                c, d, dd, v = (tok[:, 2 * z:2 * z + 2] for z in range(4))
                self.read = m = v_tt(d, self.bank.ap[:, 0:2], c, ALU.subtract, m, self.m_cd)
                m_dd = v_stt(dd, d, -1.0, d, ALU.mult, ALU.mult, m)
                md = to_diagonals(d, m)
                self.square_sums(*self.sq[0])
                m_d = on_every_partition(self.wide2, md, self.wide2.free)
                m_sq = self.square_sums(*self.sq[1])
                m_t = []

                def less_mean(t):
                    m_t.append(v_tt(t1[:, t, :], t1[:, t, :], self.wide2.ap[:, 0:S], ALU.subtract, m_d, self.sq[1][2]))

                for t in range(4):
                    less_mean(t)
                m = v_stt(v, self.bank.ap[:, 2:4], 1e-5, dd, ALU.add, ALU.add, m_sq, m_dd)
                self.bank.free = [m]
                newton = inverse_root(v, m)
                less_mean(4)
                less_mean(5)
                y, m = newton()
                md = to_diagonals(y, m)
                less_mean(6)
                less_mean(7)
                self.wide2.free = [m_t[-1]]
                mr = on_every_partition(self.wide, md, m_t[-1])
                for k in range(KT // 2):
                    s = rope_tmp.next()
                    for j in range(2):
                        t = 2 * k + j
                        m = v_tt(t1[:, t, :], t1[:, t, :], self.wide.ap[:, 0:S], ALU.mult, mr, m_t[t])
                        if self.nxt is None:
                            x_ready[t] = v_ts(x[:, t, :], t1[:, t, :], self.ln_g[:, t:t + 1], self.ln_b[:, t:t + 1], ALU.mult, ALU.add, m)
                            continue
                        m_t[t] = m
                        m = v_ts(s.ap[:, j, :], t1[:, t, :], gain_sb[:, t:t + 1], shift_sb[:, t:t + 1], ALU.mult, ALU.add, m, s.free, self.m_col)
                        split_h(t, s.ap[:, j, :], m, ends)
                    s.free = [h.marks[2 * k], h.marks[2 * k + 1]]
                self.wide.free = [V.last()]
                if self.nxt is not None:
                    for t in range(KT):
                        x_ready[t] = g_ts(x[:, t, :], t1[:, t, :], x_gain[:, t:t + 1], x_shift[:, t:t + 1], m_t[t], self.m_col)
                new_phase(ends)

        def rope(dst, bank, m_bank, cos, sin, swap, m_tab, *marks, scale=1.0):
            m = a_copy(flat(dst), bank.ap, m_bank, *marks, scale=scale)
            bank.free = [m]
            b = scratch.next()
            T.wait(m, b.free, m_tab)
            T.mm(b.ap, swap, flat(dst))
            m_sw = T.mark()
            two = lambda ap: ap.unsqueeze(1).to_broadcast([P, 2, S])
            sw = rope_tmp.next()
            m1 = v_tt(sw.ap, b.ap.rearrange("p (t n) -> p t n", t=2), two(sin), ALU.mult, m_sw, sw.free, m_tab)
            b.free = [m1]
            m2 = v_tt(dst, dst, two(cos), ALU.mult, m, m_sw)
            m3 = v_tt(dst, dst, sw.ap, ALU.add, m1, m2)
            sw.free = [m3]
            return m3

        def head_norm(o, tiles, width, eps, gains, gates, out, m_o, center=False, more=1.0):
            per = max(width, 2)
            for t in range(0, tiles, 2):
                pair = flat(o[:, t:t + 2, :])
                n = S if width == 2 else 2 * S

                def mean_of(src, m_src):
                    b = scratch.next()
                    T.wait(b.free, m_src)
                    if width == 2:
                        T.mm(b.ap[:, 0:S], con("mean_h"), src[:, 0:S], stop=False)
                        T.mm(b.ap[:, 0:S], con("mean_h"), src[:, S:2 * S], start=False)
                    else:
                        T.mm(b.ap, con("mean_h"), src)
                    return b, T.mark()

                m = m_o[t:t + 2]
                if center:
                    b, mm = mean_of(pair, m)
                    m = v_tt(pair, pair, b.ap, ALU.subtract, mm, m)
                    b.free = [m]
                    m = [m]
                sq = rope_tmp.next()
                ms = a_act(flat(sq.ap), pair, ACT.Square, m, sq.free)
                b, mm = mean_of(flat(sq.ap), ms)
                m1, m2 = rstd(flat(sq.ap)[:, 0:n], b.ap[:, 0:n], eps, mm, scale=1.0 / width)
                b.free = [m1]
                for k in (t, t + 1):
                    r = sq.ap[:, 0 if width == 2 else k - t, :]
                    mk = v_tt(o[:, k, :], o[:, k, :], r, ALU.mult, m2, m)
                    if k == t + 1:
                        sq.free = [mk]
                    if gates is None:
                        mk = v_ts(o[:, k, :], o[:, k, :], gains(k), more, ALU.mult, ALU.mult, mk)
                    else:
                        mk = v_stt(o[:, k, :], o[:, k, :], gains(k), gates[0][:, k, :], ALU.mult, ALU.mult, mk, gates[1][k])
                    out.marks[k] = split_into(out.hi[:, k, :], out.lo[:, k, :], o[:, k, :], mk)

        def attend(items, scores, weigh, blocks, values, p_ring, pt_ring, between={}):
            n = len(items)
            wts, pts = {}, {}
            for i in range(n + 3):
                if i < n:
                    bank = scratch.next()
                    T.wait(bank.free)
                    m = scores(items[i], bank)
                    slot = p_ring.next()
                    wts[i] = (slot, weigh(items[i], bank, m, slot))
                    pace(PACE_ITEM)
                if i in between:
                    between[i]()
                if 0 <= i - 2 < n:
                    slot, m = wts[i - 2]
                    bank = proj.next()
                    nb = blocks(items[i - 2])
                    T.wait(bank.free, m)
                    for b in range(nb):
                        T.turn(bank.ap[:, b * P:(b + 1) * P], slot.ap[:, b * P:(b + 1) * P], ident)
                    m = T.mark()
                    slot.free = [m]
                    pt = pt_ring.next()
                    copy = v_copy if i % 2 else a_copy
                    m = copy(pt.ap[:, 0:nb * P], bank.ap[:, 0:nb * P], m, pt.free)
                    bank.free = [m]
                    pts[i - 2] = (pt, m)
                if 0 <= i - 3 < n:
                    pt, m = pts[i - 3]
                    bank = proj.next()
                    T.wait(bank.free, m)
                    pt.free = [values(items[i - 3], bank, pt.ap)]

        def log_sigmoid(out, pre, tmp, m_pre, *marks):
            m = a_act(tmp, pre, ACT.Abs, m_pre, *marks)
            m = a_act(tmp, tmp, ACT.Exp, m, scale=-1.0)
            m = a_act(tmp, tmp, ACT.Ln, m, bias=1.0)
            return v_stt(out, pre, 0.0, tmp, ALU.min, ALU.subtract, m, m_pre)

        def carve():
            at = [0]

            def give(n, parts=P):
                ap = arena[0:parts, at[0]:at[0] + n]
                at[0] += n
                assert at[0] <= ARENA, at[0]
                return ap

            def tiles(t, n=S):
                return give(t * n).rearrange("p (t n) -> p t n", t=t)
            return give, tiles

        def cumulate(lf, lf_tm, cum, m_lf):
            b = scratch.next()
            T.wait(b.free, m_lf)
            for t in range(TT):
                T.turn(b.ap[:, 4 * t:4 * t + 4], lf[:, t * P:(t + 1) * P], ident[0:4, 0:4])
            m = T.mark()
            m = v_copy(lf_tm, b.ap[:, 0:8], m)
            b.free = [m]
            tri = con("tri").rearrange("p (u t) -> p u t", u=TT)
            b = scratch.next()
            T.wait(b.free, m)
            for u in range(TT):
                T.mm(b.ap[0:4, 0:S], lf_tm[:, 4 * u:4 * u + 4], tri[:, u, :], start=(u == 0), stop=(u == TT - 1))
            m1 = T.mark()
            m_cum = v_copy(cum, b.ap[0:4, 0:S], m1)
            b.free = [m_cum]
            return cum, m_cum, lf_tm, m

        def ffn(act, up, down, l, conv, update, need):
            give, tiles = carve()
            a_hi = [b_hi[:, i * 512:(i + 1) * 512] for i in range(3)]
            a_lo = [b_lo[:, i * 512:(i + 1) * 512] for i in range(3)]
            gated = [Slot((h, lo)) for h, lo in zip(a_hi, a_lo)]
            u_ring = Ring([give(2 * (S + 2)).rearrange("p (t n) -> p t n", t=2) for _ in range(2)])
            s_ring = Ring([tiles(2) for _ in range(3)])
            m_zero = None
            if conv:
                for s in u_ring.slots:
                    m_zero = V.do(lambda e, s=s: e.memset(s.ap[:, :, 0:2], 0.0))
            pend = []

            class Down:

                def __init__(self, i):
                    self.i, (self.slot, marks) = i, pend[i]
                    self.p = p = take(down, (l, i), hold=(i == N_UP - 1))
                    self.w_hi, self.w_lo = (w.rearrange("p (k n) -> p k n", k=2) for w in (p.hi, p.lo))
                    self.hi, self.lo = (s.rearrange("p (k n) -> p k n", k=2) for s in self.slot.ap)
                    self.marks = [p.parted, marks]
                    if i == 0:
                        self.marks += [s.free for s in scratch.slots]

                def pair(self, z):
                    i = self.i
                    T.wait(self.marks)
                    for n in (2 * z, 2 * z + 1):
                        out = banks_a[:, z, (n % 2) * S:(n % 2 + 1) * S]
                        c = slice(n * P, (n + 1) * P)
                        for k in range(2):
                            T.mm(out, self.w_hi[:, k, c], self.hi[:, k, :], start=(i == 0 and k == 0 and n % 2 == 0), stop=False, free=True)
                            T.mm(out, self.w_hi[:, k, c], self.lo[:, k, :], start=False, stop=False, free=True)
                            T.mm(out, self.w_lo[:, k, c], self.hi[:, k, :], start=False, stop=(i == N_UP - 1 and k == 1), free=True)
                    if z == KT // 2 - 1 or i == N_UP - 1:
                        m = T.mark()
                        if z == KT // 2 - 1:
                            self.slot.free = [m]
                            give_back(self.p, m)
                        return m

            def down_piece(i):
                pace()
                d = Down(i)
                for z in range(KT // 2):
                    d.pair(z)

            def last_pieces():
                one, two = Down(N_UP - 2), Down(N_UP - 1)
                for z in range(KT // 2):
                    one.pair(z)
                for z in range(KT // 2):
                    m = two.pair(z)
                    update.before(z)
                    for j in range(2):
                        m_f = update.finish(2 * z + j, banks_a[:, z, j * S:(j + 1) * S], m)
                    scratch.slots[z].free = [m_f]

            for i in range(N_UP):
                bu, mu = project(up, (l, i), act)
                s = s_ring.next()
                if conv:
                    ub = u_ring.next()
                    m = a_copy(ub.ap[:, :, 2:S + 2], bu.ap.rearrange("p (t n) -> p t n", t=2), mu, ub.free)
                    mc = [a_act(s.ap[:, j, :], bu.ap[:, j * S:(j + 1) * S], ACT.Identity, m, s.free,
                                scale=col(f"w_conv{l}", 44 + 2 * i + j), bias=col(f"b_conv{l}", 2 * i + j)) for j in range(2)]
                    bu.free = [mc[1]]
                    for j in range(2):
                        t = 2 * i + j
                        w = [col(f"w_conv{l}", 22 * q + t) for q in range(2)]
                        mj = mc[j]
                        mj = v_stt(s.ap[:, j, :], ub.ap[:, j, 1:S + 1], w[1], s.ap[:, j, :], ALU.mult, ALU.add, mj, m_zero)
                        mj = v_stt(s.ap[:, j, :], ub.ap[:, j, 0:S], w[0], s.ap[:, j, :], ALU.mult, ALU.add, mj)
                    ub.free = [mj]
                else:
                    m = a_act(flat(s.ap), bu.ap, ACT.Silu, mu, s.free)
                    bu.free = [m]
                bg, mg = project(up, (l, N_UP + i), act)
                if conv:
                    m = a_act(flat(s.ap), flat(s.ap), ACT.Silu, mj)
                m = v_tt(flat(s.ap), flat(s.ap), bg.ap, ALU.mult, m, mg)
                bg.free = [m]
                slot = gated[i % 3]
                marks = split_into(slot.ap[0], slot.ap[1], flat(s.ap), m, slot.free)
                s.free = list(marks)
                pend.append((slot, marks))
                if 1 <= i < N_UP - 1:
                    down_piece(i - 1)
            ada_until(*need)
            update.columns()
            last_pieces()
            update.end()

        b_hi3 = b_hi.rearrange("p (t n) -> p t n", n=S)
        b_lo3 = b_lo.rearrange("p (t n) -> p t n", n=S)
        HD = P ** -0.5

        def out_project(name, out, update, *idx):
            update.columns()
            for c in range(4):
                b, m = project(name, (*idx, c), out, last=(c == 3))
                update.before(c)
                for j in range(2):
                    mf = update.finish(2 * c + j, b.ap[:, j * S:(j + 1) * S], m)
                b.free = [mf]
            update.end()

        first = ToRms(proj, None, ("norm1_g0", 0), 0, 0)
        ada_until(0, 3)
        for k in range(KT // 2):
            first.before(k)
        first_root = first.root()
        ada_until(0, 8)
        m_c1 = load(c1[:, 0:a["const1"].shape[1]], "const1")
        rows = c0[64:65, where0["pick"][0]:where0["pick"][0] + 1024]
        m_lam = load(rows[:, 0:256], "lam", m_c0)
        m_sink = load(rows[:, 256:272], "sinks", m_c0)
        m_a2 = []
        wa2_sb = c0[32:49, where0["pick"][0]:where0["pick"][0] + 512]
        for l in range(2):
            m_a2.append(load(wa2_sb[:, l * 256:(l + 1) * 256], f"wa2{l}", m_c0))
        pos_i = rows[:, 512:512 + S].bitcast(I32)
        m_pos = load(pos_i, "pos", m_c0)
        first.columns()
        first.end(first_root)
        st["ahead"] = AHEAD
        for l in range(2):
            branch = [Split(b_hi3[:, 4 * n:4 * n + 4, :], b_lo3[:, 4 * n:4 * n + 4, :], 4) for n in range(3)]
            give, tiles = carve()
            qa, ka, va = tiles(4), tiles(4), tiles(TT, 512)
            ga = tiles(4)
            qb, kb, vb = tiles(2), tiles(TT), tiles(TT, 512)
            o = t1[:, 0:4, :]
            gb = t1[:, 4:8, :]
            misc = give(1024)
            P_all = give(4 * S)
            P_ring = Ring([P_all[:, z * S:(z + 1) * S] for z in range(4)])
            PT_ring = Ring([give(S) for _ in range(3)])
            cosr, sinr, swapr = con("cos128"), con("sin128"), con("swap128")
            m_q, m_k, m_v, m_g = [None] * 2, [None] * 2, [None] * 2, [None] * 4

            def to_tokens(dst, i0, n, marks):
                for j in range(n):
                    b, m = project("w_in", (l, i0 + j), h, tm=True)
                    marks[j] = v_copy(dst[:, :, j * PC:(j + 1) * PC], b.ap.rearrange("p (t n) -> p t n", t=TT), m)
                    b.free = [marks[j]]

            def to_gates(dst, i0, n, marks, *after):
                for j in range(n):
                    b, m = project("w_in", (l, i0 + j), h)
                    m = a_act(flat(dst[:, 2 * j:2 * j + 2, :]), b.ap, ACT.Silu, m, *after)
                    b.free = [m]
                    marks[2 * j] = marks[2 * j + 1] = m

            for j in range(2):
                b, m = project("w_in", (l, j), h)
                m_q[j] = rope(qa[:, 2 * j:2 * j + 2, :], b, m, cosr, sinr, swapr, m_c1)
            for j in range(2):
                b, m = project("w_in", (l, 2 + j), h)
                m_k[j] = rope(ka[:, 2 * j:2 * j + 2, :], b, m, cosr, sinr, swapr, m_c1)
            to_tokens(va, 4, 2, m_v)
            to_gates(ga, 6, 2, m_g)
            p = take("w_in_s", (l,), KT * P)
            bank = proj.next()
            m = gemm_fm(p, h, bank, n_tiles=1, width=P)
            ff, low = misc[0:4, 0:S], misc[32:49, S:2 * S]
            m1 = a_act(ff, bank.ap[0:4, 0:S], ACT.Identity, m, bias=col(f"b_fox_f{l}")[0:4, :])
            m2 = V.do(lambda e: e.memset(low, 1.0))
            m_low = v_copy(low[0:16, :], bank.ap[32:48, 0:S], m1, m2)
            bank.free = [m1, m_low]
            m_ff = m1
            b, m = project("w_in", (l, 8), h)
            m_qb = a_copy(flat(qb), b.ap, m, scale=64 ** -0.5)
            b.free = [m_qb]
            b, m = project("w_in", (l, 9), h, tm=True)
            m_kb = v_copy(flat(kb), b.ap, m)
            b.free = [m_kb]
            m_vb = [None] * 2
            to_tokens(vb, 10, 2, m_vb)

            m_o = [None] * 4
            decay = con("ret_decay").rearrange("p (h n) -> p h n", h=HEADS)
            w_ring = Ring([give(3 * P) for _ in range(2)])

            def ret_scores(hd):
                b = scratch.next()
                T.wait(b.free, m_q[hd // 2], m_k[hd // 2])
                T.mm(b.ap[:, 0:S], ka[:, hd, 0:P], qa[:, hd, :])
                T.mm(b.ap[:, S:S + P], ka[:, hd, P:S], qa[:, hd, P:S])
                m = T.mark()
                w = w_ring.next()
                m = v_tt(w.ap, b.ap[:, 0:3 * P], decay[:, hd, :], ALU.mult, m, w.free, m_c1)
                b.free = [m]
                return w, m

            def ret_values(hd, w, m):
                b = scratch.next()
                T.wait(b.free, m, m_v)
                c = slice(hd * P, (hd + 1) * P)
                T.mm(b.ap[:, 0:P], va[:, 0, c], w.ap[:, 0:P])
                T.mm(b.ap[:, P:S], va[:, 0, c], w.ap[:, P:2 * P], stop=False)
                T.mm(b.ap[:, P:S], va[:, 1, c], w.ap[:, 2 * P:3 * P], start=False)
                m = T.mark()
                w.free = [m]
                m_o[hd] = a_copy(o[:, hd, :], b.ap[:, 0:S], m)
                b.free = [m_o[hd]]

            A.wait(h.marks)
            V.wait(h.marks)
            T.wait(h.marks)
            prev = None
            for hd in range(HEADS):
                cur = (hd, *ret_scores(hd))
                if prev:
                    ret_values(*prev)
                prev = cur
            ret_values(*prev)
            head_norm(o, 4, 1, 1e-6, lambda k: col(f"ret_norm_g{l}", k), (ga, m_g), branch[0], m_o, center=True)

            bank = scratch.next()
            T.wait(bank.free, m_low, m_a2[l])
            for t in range(TT):
                T.mm(bank.ap[:, t * 256:(t + 1) * 256], low[:, t * P:(t + 1) * P], wa2_sb[:, l * 256:(l + 1) * 256])
            m = T.mark()
            la, tmp = give(512), give(512)
            m_la = log_sigmoid(la, bank.ap, tmp, m)
            bank.free = [m_la]
            m_lf = log_sigmoid(misc[0:4, 0:S], ff, misc[0:4, 512:512 + S], m_ff)
            to_gates(gb, 12, 2, m_g)
            bank = scratch.next()
            T.wait(bank.free, m_la)
            T.mm(bank.ap, con("gla_suffix"), la)
            m = T.mark()
            m = a_act(tmp, bank.ap, ACT.Exp, m, m_la)
            bank.free = [m]
            m_kd = v_tt(flat(kb), flat(kb), tmp, ALU.mult, m, m_kb)
            bank = scratch.next()
            T.wait(bank.free)
            for hp in range(2):
                for t in range(TT):
                    T.mm(bank.ap[:, 4 * hp + 2 * t:4 * hp + 2 * t + 2], la[:, t * 256 + hp * P:t * 256 + hp * P + P], con("gla_chunk"))
            m = T.mark()
            a_chunk = small[:, 32:40]
            m_ac = a_act(a_chunk, bank.ap[:, 0:8], ACT.Exp, m)
            bank.free = [m_ac]
            cum, m_cum, _, _ = cumulate(misc[0:4, 0:S], give(8), misc[0:4, 3 * S:4 * S], m_lf)
            states = P_all.rearrange("p (t n) -> p t n", n=P)
            m_st = [None] * 8
            for n in range(4):
                r = slice(64 * (n % 2), 64 * (n % 2) + 64)
                bank = scratch.next()
                T.wait(bank.free, m_kd, m_vb)
                for hp in range(2):
                    for e in range(2):
                        hd = 2 * hp + e
                        T.mm(bank.ap[64 * e:64 * e + 64, hp * P:(hp + 1) * P], kb[r, n // 2, hd * 64:(hd + 1) * 64],
                             vb[r, n // 2, hd * P:(hd + 1) * P])
                m = T.mark()
                for hp in range(2):
                    if n == 0:
                        m_st[hp] = v_copy(states[:, hp, :], bank.ap[:, hp * P:(hp + 1) * P], m)
                    else:
                        m_st[2 * n + hp] = v_stt(states[:, 2 * n + hp, :], states[:, 2 * n - 2 + hp, :],
                                                 a_chunk[:, 4 * hp + n:4 * hp + n + 1], bank.ap[:, hp * P:(hp + 1) * P],
                                                 ALU.mult, ALU.add, m, m_ac, m_st[2 * n - 2 + hp])
                bank.free = [m_st[2 * n + 1]]

            A.wait(branch[0].marks)
            for hd in range(HEADS):
                bank = scratch.next()
                r = slice(64 * (hd % 2), 64 * (hd % 2) + 64)
                T.wait(bank.free, m_qb, m_st)
                for n in range(4):
                    T.mm(bank.ap[:, n * 64:(n + 1) * 64], states[r, 2 * n + hd // 2, :], qb[r, hd // 2, n * 64:(n + 1) * 64])
                m = T.mark()
                m_o[hd] = a_copy(o[:, hd, :], bank.ap[:, 0:S], m)
                bank.free = [m_o[hd]]
            for z in P_ring.slots:
                z.free = [m, m_st]
            head_norm(o, 4, 1, 1e-6, lambda k: col(f"gla_norm_g{l}"), (gb, m_g), branch[1], m_o)

            for which, (dst, i0) in enumerate(((qa, 14), (ka, 16))):
                gain = small[:, 40 + which:41 + which]
                m_gn = v_ts(gain, col(f"q_norm_g{l}" if which == 0 else f"k_norm_g{l}"), HD if which == 0 else 1.0, None, ALU.mult, None, V.last(), T.last())
                for j in range(2):
                    b, m = project("w_in", (l, i0 + j), h)
                    d2 = dst[:, 2 * j:2 * j + 2, :]
                    sq = rope_tmp.next()
                    m_sq = a_act(flat(sq.ap), b.ap, ACT.Square, m, sq.free)
                    m_cp = v_copy(flat(d2), b.ap, m_sq)
                    b.free = [m_cp, m_sq]
                    b2 = scratch.next()
                    T.wait(b2.free, m_sq)
                    T.mm(b2.ap, con("mean_h"), flat(sq.ap))
                    m = T.mark()
                    m, m_r = rstd(flat(sq.ap), b2.ap, 1e-6, m)
                    b2.free = [m]
                    m = v_stt(flat(d2), flat(d2), gain, flat(sq.ap), ALU.mult, ALU.mult, m_cp, m_r, m_gn)
                    sq.free = [m]
                    (m_q if which == 0 else m_k)[j] = m
            to_tokens(va, 18, 2, m_v)
            pick = con("pick")[0:4, :].rearrange("p (h n) -> p h n", h=HEADS)
            unpick = con("unpick")[0:4, :].rearrange("p (h n) -> p h n", h=HEADS)
            A.wait(branch[1].marks)
            stats = small[:, 48:96]

            def fox_scores(it, bank):
                hd, t, i = it
                nk = (t + 1) * P
                out = bank.ap[:, 0:nk]
                T.wait(m_q[hd // 2], m_k[hd // 2], m_cum)
                T.mm(out, qa[:, hd, t * P:(t + 1) * P], ka[:, hd, 0:nk], stop=False)
                T.mm(out, cum[:, t * P:(t + 1) * P], pick[:, hd, 0:nk], start=False, stop=False)
                T.mm(out, unpick[:, hd, :], cum[:, 0:nk], start=False, stop=False)
                T.mm(bank.ap[:, nk - P:nk], ident, con("mask_after"), start=False)
                return T.mark()

            def fox_weigh(it, bank, m, slot):
                hd, t, i = it
                nk = (t + 1) * P
                nm, rs, ri = (stats[:, 3 * (i % 8) + k:3 * (i % 8) + k + 1] for k in range(3))
                m = V.do(lambda e: e.tensor_reduce(nm, bank.ap[:, 0:nk], AX, ALU.max, negate=True), m)
                m = a_act(slot.ap[:, 0:nk], bank.ap[:, 0:nk], ACT.Exp, m, slot.free, bias=nm, accum=rs)
                bank.free = [m]
                m = v_recip(ri, rs, m)
                return v_ts(slot.ap[:, 0:nk], slot.ap[:, 0:nk], ri, None, ALU.mult, None, m)

            def fox_values(it, bank, pt):
                hd, t, i = it
                c = slice(hd * P, (hd + 1) * P)
                T.wait(m_v)
                for b in range(t + 1):
                    T.mm(bank.ap[:, 0:P], va[:, b, c], pt[:, b * P:(b + 1) * P], start=(b == 0), stop=(b == t))
                m = T.mark()
                m_o[hd] = a_copy(o[:, hd, t * P:(t + 1) * P], bank.ap[:, 0:P], m)
                bank.free = [m_o[hd]]
                if t == TT - 1:
                    branch[2].marks[hd] = split_into(branch[2].hi[:, hd, :], branch[2].lo[:, hd, :], o[:, hd, :], m_o[hd])
                return m

            items = [(hd, t, 2 * hd + t) for hd in range(HEADS) for t in range(TT)]
            attend(items, fox_scores, fox_weigh, lambda it: it[1] + 1, fox_values, P_ring, PT_ring)

            new_phase()
            give, tiles = carve()
            g_ring = Ring([tiles(2) for _ in range(3)])
            m_mix = [None] * 4
            for c in range(4):
                mix = flat(t1[:, 2 * c:2 * c + 2, :])
                for n in range(3):
                    b, m = project("w_mg", (l, 4 * n + c), h)
                    g = g_ring.next()
                    for j in range(2):
                        mg = a_act(g.ap[:, j, :], b.ap[:, j * S:(j + 1) * S], ACT.Sigmoid, m, g.free, bias=col(f"b_mg{l}", 8 * n + 2 * c + j))
                    b.free = [mg]
                    pace()
                    p = take("w_br", (l, n, c), 4 * PC)
                    b = proj.next()
                    m = gemm_fm(p, branch[n], b, kts=4)
                    if n == 0:
                        m_mix[c] = v_tt(mix, flat(g.ap), b.ap, ALU.mult, m, mg)
                        b.free = g.free = [m_mix[c]]
                    else:
                        m = v_tt(flat(g.ap), flat(g.ap), b.ap, ALU.mult, m, mg)
                        b.free = [m]
                        m_mix[c] = G.do(lambda e, mix=mix, g=g: e.tensor_tensor(mix, mix, flat(g.ap), ALU.add), m, m_mix[c])
                        g.free = [m_mix[c]]
            m_h = T.last()
            mixed = Split(h_hi, h_lo, KT)
            for t in range(KT):
                mixed.marks[t] = split_into(h_hi[:, t, :], h_lo[:, t, :], t1[:, t, :], m_mix[t // 2], m_h)
            ada_until(l, 20)
            out_project("w_o", mixed, ToRms(scratch, mod[:, MOD[l] + 16:MOD[l] + 24], (f"norm2_g{l}", 0), l, 1, mod_mark[l]), l)
            ada_until(l)
            gate = mod[:, MOD[l] + 40:MOD[l] + 48]
            if l == 0:
                nxt = ToRms(proj, gate, ("norm1_g1", 0), 1, 0, mod_mark[l])
            else:
                nxt = ToPlain(proj, gate, 2, mod_mark[l])
            ffn(h, "w_up", "w_down", l, True, nxt, (l + 1, 8))

        m_c3 = load(c1[:, 0:a["const3"].shape[1]], "const3", *everyone())
        give, tiles = carve()
        posf = give(S)[64:65, :]
        m = v_copy(posf, pos_i, m_pos)
        bank = scratch.next()
        T.wait(bank.free, m)
        T.mm(bank.ap[:, 0:S], ones[64:65, :], posf)
        m = T.mark()
        ang, turns, red = give(S), give(S), give(S)
        m_ang = v_ts(ang, bank.ap[:, 0:S], con("inv16"), None, ALU.mult, None, m)
        bank.free = [m_ang]
        MAGIC = float(1.5 * 2 ** 23)
        C1 = 6.28125
        C2 = float(np.float32(TWO_PI - C1))
        C3 = float(np.float32(TWO_PI - C1 - C2))
        for k, quarter in ((0, 0.25), (1, 0.0)):
            m = v_ts(turns, ang, 1 / TWO_PI, quarter, ALU.mult, ALU.add, m_ang, A.last())
            m = v_ts(turns, turns, MAGIC, None, ALU.add, None, m)
            m = v_ts(turns, turns, MAGIC, None, ALU.subtract, None, m)
            m = v_stt(red, turns, -C1, ang, ALU.mult, ALU.add, m, A.last())
            m = v_stt(red, turns, -C2, red, ALU.mult, ALU.add, m)
            m = v_stt(red, turns, -C3, red, ALU.mult, ALU.add, m)
            m = v_ts(red, red, quarter * TWO_PI, 3.1415925, ALU.add, ALU.min, m)
            m = v_ts(red, red, -3.1415925, None, ALU.max, None, m)
            m_rope = a_act(rope16[:, k, :], red, ACT.Sin, m)
        cos16, sin16 = rope16[:, 0, :], rope16[:, 1, :]
        bank = scratch.next()
        T.wait(bank.free, m_sink)
        T.mm(bank.ap[:, 0:16], ones[64:65, :], rows[:, 256:272])
        m = T.mark()
        sinks, unsinks = small[:, 96:112], small[:, 112:128]
        m1 = v_copy(sinks, bank.ap[:, 0:16], m)
        m_sinks = v_ts(unsinks, bank.ap[:, 0:16], -1.0, None, ALU.mult, None, m)
        bank.free = [m_sinks]
        LAM_INIT = 0.8 - 0.6 * math.exp(-0.3 * 3)
        lam4 = rows[:, 0:256].rearrange("p (a b n) -> p a b n", a=2, b=2)
        prod = rows[:, 272:400].rearrange("p (a n) -> p a n", a=2)
        m = v_tt(prod, lam4[:, :, 0, :], lam4[:, :, 1, :], ALU.mult, m_lam)
        m = V.do(lambda e: e.tensor_reduce(rows[:, 400:402], prod, AX, ALU.add), m)
        m = a_act(rows[:, 402:404], rows[:, 400:402], ACT.Exp, m)
        m = v_tt(rows[:, 404:405], rows[:, 403:404], rows[:, 402:403], ALU.subtract, m)
        m = v_ts(rows[:, 404:405], rows[:, 404:405], -LAM_INIT, None, ALU.add, None, m)
        bank = scratch.next()
        T.wait(bank.free, m)
        T.mm(bank.ap[:, 0:1], ones[64:65, :], rows[:, 404:405])
        m = T.mark()
        neg_lam = small[:, 24:25]
        m_nl = v_copy(neg_lam, bank.ap[:, 0:1], m)
        bank.free = [m_nl]

        def to_tokens2(name, dst, i0, n, marks, first=0):
            for j in range(first, first + n):
                b, m = project(name, (i0 + j,), h, tm=True)
                marks.append(v_copy(dst[:, :, j * PC:(j + 1) * PC], b.ap.rearrange("p (t n) -> p t n", t=TT), m))
                b.free = [marks[-1]]

        y_split = Split(b_hi3[:, 0:8, :], b_lo3[:, 0:8, :], KT)

        def mlstm():
            give, tiles = carve()
            q, k, v = tiles(4), tiles(4), tiles(TT, D)
            o = t1
            m_q, m_k, m_v = [], [], []
            for dst, i0, marks, sc in ((q, 0, m_q, HD), (k, 2, m_k, 1.0)):
                for j in range(2):
                    b, m = project("mlstm_in", (i0 + j,), h)
                    marks.append(a_copy(flat(dst[:, 2 * j:2 * j + 2, :]), b.ap, m, scale=sc))
                    b.free = [marks[-1]]
            p = take("mlstm_in_s", (0,), KT * P)
            bank = proj.next()
            m = gemm_fm(p, h, bank, n_tiles=1, width=P)
            ig, fp, fpre = give(S)[0:4, :], give(S)[0:4, :], give(S)[0:36, :]
            m_i = a_act(ig, bank.ap[0:4, 0:S], ACT.Identity, m, bias=col("b_gate")[0:4, :])
            m_f0 = a_act(fpre[32:36, :], bank.ap[32:36, 0:S], ACT.Identity, m, bias=col("b_gate")[32:36, :])
            bank.free = [m_f0]
            m_f0 = v_copy(fp, fpre[32:36, :], m_f0)
            tmp = give(S)[0:4, :]
            m_lf = log_sigmoid(fp, fp, tmp, m_f0)
            to_tokens2("mlstm_in", v, 4, 2, m_v)
            cum, m_cum, lf_tm, m_lt = cumulate(fp, give(8), give(S)[0:4, :], m_lf)
            m_gi = v_tt(ig, ig, cum, ALU.subtract, m_i, m_cum)
            tri = con("tri").rearrange("p (u t) -> p u t", u=TT)
            bank = scratch.next()
            T.wait(bank.free, m_lt)
            for t in range(TT):
                for u in range(t + 1):
                    T.mm(bank.ap[:, 4 * t:4 * t + 4], tri[:, u, t * P:(t + 1) * P], lf_tm[:, 4 * u:4 * u + 4], start=(u == 0), stop=(u == t))
            m = T.mark()
            nb_tm = small[:, 32:40]
            m_nb = v_ts(nb_tm, bank.ap[:, 0:8], -1.0, None, ALU.mult, None, m)
            bank.free = [m_nb]
            pick = con("pick")[0:4, :].rearrange("p (h n) -> p h n", h=HEADS)
            stats = small[:, 48:96]
            W_ring = Ring([give(S) for _ in range(4)])
            P_ring = Ring([give(S) for _ in range(4)])
            PT_ring = Ring([give(S) for _ in range(3)])
            m_o = [None] * 8
            A.wait(h.marks, x_ready)

            def scores(it, bank):
                hd, t, i = it
                nk = (t + 1) * P
                T.wait(m_q[hd // 2], m_k[hd // 2], m_gi, m_cum)
                T.mm(bank.ap[:, 0:nk], q[:, hd, t * P:(t + 1) * P], k[:, hd, 0:nk])
                out = bank.ap[:, S:S + nk]
                T.mm(out, cum[:, t * P:(t + 1) * P], pick[:, hd, 0:nk], stop=False)
                T.mm(out, pick[:, hd, 0:P], ig[:, 0:nk], start=False, stop=False)
                T.mm(bank.ap[:, S + nk - P:S + nk], ident, con("mask_after"), start=False)
                return T.mark()

            def weigh(it, bank, m, slot):
                hd, t, i = it
                nk = (t + 1) * P
                c = 4 * (i % 8)
                nm0, nm, den, em = (stats[:, c + z:c + z + 1] for z in range(4))
                w = W_ring.next()
                m1 = V.do(lambda e: e.tensor_reduce(nm0, bank.ap[:, S:S + nk], AX, ALU.max, negate=True), m)
                m1 = v_tt(nm, nm0, nb_tm[:, 4 * t + hd:4 * t + hd + 1], ALU.min, m1, m_nb)
                m2 = a_act(w.ap[:, 0:nk], bank.ap[:, S:S + nk], ACT.Exp, m1, w.free, bias=nm)
                m3 = a_act(em, nm, ACT.Exp, m1)
                m2 = V.do(lambda e: e.tensor_tensor_reduce(slot.ap[:, 0:nk], bank.ap[:, 0:nk], w.ap[:, 0:nk], 1.0, 0.0,
                                                           ALU.mult, ALU.add, den), m2, slot.free)
                bank.free = w.free = [m2]
                m4 = v_ts(nm0, den, -1.0, None, ALU.mult, None, m2)
                m4 = v_tt(den, den, nm0, ALU.max, m4)
                m4 = v_tt(den, den, em, ALU.max, m4, m3)
                m4 = v_recip(den, den, m4)
                return v_ts(slot.ap[:, 0:nk], slot.ap[:, 0:nk], den, None, ALU.mult, None, m4)

            def values(it, bank, pt):
                hd, t, i = it
                T.wait(m_v)
                for e in range(2):
                    c = slice(hd * S + e * P, hd * S + (e + 1) * P)
                    for b in range(t + 1):
                        T.mm(bank.ap[:, e * P:(e + 1) * P], v[:, b, c], pt[:, b * P:(b + 1) * P], start=(b == 0), stop=(b == t))
                m = T.mark()
                mo = a_copy(o[:, 2 * hd:2 * hd + 2, t * P:(t + 1) * P], bank.ap[:, 0:S].rearrange("p (e n) -> p e n", e=2), m)
                m_o[2 * hd] = m_o[2 * hd + 1] = mo
                bank.free = [mo]
                return m

            items = [(hd, t, 2 * hd + t) for hd in range(HEADS) for t in range(TT)]
            g, m_g = tiles(8), [None] * 8

            def v_piece(j):
                to_tokens2("mlstm_in", v, 4, 1, m_v, j)

            def g_piece(j):
                b, m = project("mlstm_in", (8 + j,), h)
                b.free = [v_copy(pair(g, j), b.ap, m)]
                m_g[2 * j] = m_g[2 * j + 1] = b.free[0]

            between = {1: lambda: v_piece(2), 3: lambda: v_piece(3)}
            between.update({5 + j: (lambda j=j: g_piece(j)) for j in range(4)})
            attend(items, scores, weigh, lambda it: it[1] + 1, values, P_ring, PT_ring, between)
            for j in range(4):
                m_g[2 * j] = m_g[2 * j + 1] = a_act(pair(g, j), pair(g, j), ACT.Sigmoid, m_g[2 * j])
            head_norm(o, 8, 2, 1e-6, lambda n: col("mlstm_norm", n), (g, m_g), y_split, m_o)
            return "mlstm_out", y_split

        def swa():
            give, tiles = carve()
            q, k, v = tiles(8), tiles(2), tiles(TT, P)
            o, m_o = t1, [None] * 8
            m_q, m_k = [], []

            def q_piece(j):
                b, m = project("swa_in", (j,), h)
                m_q.append(rope(q[:, 2 * j:2 * j + 2, :], b, m, cos16, sin16, con("swap16"), m_rope))

            q_piece(0)
            p = take("swa_in", (4,))
            bank = proj.next()
            T.wait(bank.free, p.parted)
            w_hi, w_lo = (w.rearrange("p (k n) -> p k n", k=KT) for w in (p.hi, p.lo))
            for n in range(3):
                out = bank.ap[:, 0:S] if n == 0 else bank.ap[:, S + (n - 1) * P:S + n * P]
                r = slice((n - 1) * P, n * P)
                for kk in range(KT):
                    T.wait(h.marks[kk])
                    if n == 0:
                        three = [(w_hi[:, kk, 0:P], h.hi[:, kk, :]), (w_hi[:, kk, 0:P], h.lo[:, kk, :]), (w_lo[:, kk, 0:P], h.hi[:, kk, :])]
                    else:
                        three = [(h.hi[:, kk, r], w_hi[:, kk, P:]), (h.hi[:, kk, r], w_lo[:, kk, P:]), (h.lo[:, kk, r], w_hi[:, kk, P:])]
                    for z, (lt, rt) in enumerate(three):
                        T.mm(out, lt, rt, start=(kk == 0 and z == 0), stop=(kk == KT - 1 and z == 2))
            m = T.mark()
            give_back(p, m)
            kk_ = give(S)
            mk = a_copy(kk_, bank.ap[:, 0:S], m)
            m_v = v_copy(flat(v), bank.ap[:, S:2 * S], mk)
            bank.free = [m_v]
            b = scratch.next()
            T.wait(b.free, mk, m_rope)
            T.mm(b.ap[:, 0:S], con("swap16"), kk_)
            m_sw = T.mark()
            sw = rope_tmp.next()
            m1 = v_tt(sw.ap[:, 0, :], b.ap[:, 0:S], sin16, ALU.mult, m_sw, sw.free)
            b.free = [m1]
            m2 = v_tt(kk_, kk_, cos16, ALU.mult, mk, m_sw)
            m3 = v_tt(kk_, kk_, sw.ap[:, 0, :], ALU.add, m1, m2)
            sw.free = [m3]
            for kv in range(2):
                for half in range(2):
                    m_k.append(v_copy(k[64 * half:64 * half + 64, kv, :], kk_[64 * kv:64 * kv + 64, :], m3))
            stats = small[:, 48:96]
            P_ring = Ring([give(S) for _ in range(4)])
            PT_ring = Ring([give(S) for _ in range(3)])
            A.wait(h.marks, x_ready)
            V.wait(h.marks, x_ready)
            SC = 64 ** -0.5

            def scores(it, bank):
                hd, t, i = it
                nk = (t + 1) * P
                r = slice(64 * (hd % 2), 64 * (hd % 2) + 64)
                T.wait(m_q[hd // 4], m_k)
                T.mm(bank.ap[:, 0:nk], q[r, hd // 2, t * P:(t + 1) * P], k[r, hd // 8, 0:nk], stop=False)
                if t == 1:
                    T.mm(bank.ap[:, 0:P], ident, con("mask_band"), start=False, stop=False)
                T.mm(bank.ap[:, nk - P:nk], ident, con("mask_after"), start=False)
                return T.mark()

            def weigh(it, bank, m, slot):
                hd, t, i = it
                nk = (t + 1) * P
                c = 4 * (i % 8)
                m0, nm, rs, es = (stats[:, c + z:c + z + 1] for z in range(4))
                m = V.do(lambda e: e.tensor_reduce(m0, bank.ap[:, 0:nk], AX, ALU.max), m)
                m1 = v_ts(nm, m0, -SC, unsinks[:, hd:hd + 1], ALU.mult, ALU.min, m, m_sinks)
                m = a_act(slot.ap[:, 0:nk], bank.ap[:, 0:nk], ACT.Exp, m1, slot.free, bias=nm, scale=SC, accum=rs)
                bank.free = [m]
                m2 = a_act(es, sinks[:, hd:hd + 1], ACT.Exp, m1, m_sinks, bias=nm)
                m = v_tt(rs, rs, es, ALU.add, m, m2)
                m = v_recip(rs, rs, m)
                return v_ts(slot.ap[:, 0:nk], slot.ap[:, 0:nk], rs, None, ALU.mult, None, m)

            def values(it, bank, pt):
                hd, t, i = it
                r = slice(64 * (hd % 2), 64 * (hd % 2) + 64)
                c = slice(64 * (hd // 8), 64 * (hd // 8) + 64)
                T.wait(m_v)
                for b in range(t + 1):
                    T.mm(bank.ap[r, 0:P], v[:, b, c], pt[:, b * P:(b + 1) * P], start=(b == 0), stop=(b == t))
                m = T.mark()
                mo = a_copy(o[r, hd // 2, t * P:(t + 1) * P], bank.ap[r, 0:P], m)
                bank.free = [mo]
                if t == TT - 1 and hd % 2:
                    n = hd // 2
                    y_split.marks[n] = split_into(y_split.hi[:, n, :], y_split.lo[:, n, :], o[:, n, :], mo)
                return m

            items = [(hd, t, 2 * hd + t) for hd in range(16) for t in range(TT)]
            attend(items, scores, weigh, lambda it: it[1] + 1, values, P_ring, PT_ring,
                   {8 * j - 5: (lambda j=j: q_piece(j)) for j in range(1, 4)})
            return "swa_out", y_split

        def hgrn():
            give, tiles = carve()
            NH = 8
            q, k, v, lf_tm = tiles(8), tiles(8), tiles(TT, D), tiles(TT, D)
            lbs = col("hgrn_lb", 0, 32).rearrange("p (l t) -> p l t", l=4)
            mx, ex = give(8), give(32)
            ex4 = ex.rearrange("p (l t) -> p l t", l=4)
            lb, omlb = give(8), give(8)
            m = v_tt(mx, lbs[:, 0, :], lbs[:, 1, :], ALU.max)
            m = v_tt(mx, mx, lbs[:, 2, :], ALU.max, m)
            m = v_tt(mx, mx, lbs[:, 3, :], ALU.max, m)
            m = v_tt(ex4, lbs, mx.unsqueeze(1).to_broadcast([P, 4, 8]), ALU.subtract, m)
            m_e = a_act(ex, ex, ACT.Exp, m)
            m = v_tt(lb, ex4[:, 1, :], ex4[:, 2, :], ALU.add, m_e)
            m1 = v_tt(omlb, ex4[:, 0, :], ex4[:, 3, :], ALU.add, m_e)
            m2 = v_tt(mx, lb, omlb, ALU.add, m, m1)
            m2 = v_recip(mx, mx, m2)
            m_lb = v_tt(lb, lb, mx, ALU.mult, m2)
            m_lb = v_tt(omlb, omlb, mx, ALU.mult, m_lb)
            m_q, m_k, m_v, m_lt = [], [], [], []
            V.wait(h.marks, x_ready)
            A.wait(h.marks, x_ready)
            for j in range(4):
                b, m = project("hgrn_in", (4 + j,), h)
                f2, k2 = t1[:, 2 * j:2 * j + 2, :], k[:, 2 * j:2 * j + 2, :]
                m1 = a_act(flat(f2), b.ap, ACT.Sigmoid, m)
                m2 = a_act(flat(k2), b.ap, ACT.Sigmoid, m, scale=-1.0)
                b.free = [m2]
                for e in range(2):
                    n = 2 * j + e
                    m3 = v_ts(f2[:, e, :], f2[:, e, :], omlb[:, n:n + 1], lb[:, n:n + 1], ALU.mult, ALU.add, m1, m_lb)
                    mk = v_ts(k2[:, e, :], k2[:, e, :], omlb[:, n:n + 1], None, ALU.mult, None, m2)
                m_k.append(mk)
                m3 = v_ts(flat(f2), flat(f2), 2.0 ** -60, None, ALU.max, None, m3)
                m_k[-1] = mk
                m_lt.append(m3)
            for j in range(4):
                f2 = t1[:, 2 * j:2 * j + 2, :]
                m3 = a_act(flat(f2), flat(f2), ACT.Ln, m_lt[j])
                b = scratch.next()
                T.wait(b.free, m3)
                for t in range(TT):
                    for e in range(2):
                        T.turn(b.ap[:, (2 * t + e) * P:(2 * t + e + 1) * P], f2[:, e, t * P:(t + 1) * P], ident)
                m = T.mark()
                m_lt[j] = v_copy(lf_tm[:, :, j * PC:(j + 1) * PC], b.ap.rearrange("p (t n) -> p t n", t=TT), m)
                b.free = [m_lt[j]]
            for j in range(4):
                b, m = project("hgrn_in", (j,), h)
                m_q.append(a_copy(flat(q[:, 2 * j:2 * j + 2, :]), b.ap, m))
                b.free = [m_q[-1]]
            to_tokens2("hgrn_in", v, 8, 4, m_v)
            decay = con("hg_decay").rearrange("p (l n) -> p l n", l=9)
            mask = con("hg_mask")
            pairs = Ring([banks_a[:, 2 * z:2 * z + 2, :].rearrange("p a n -> p (a n)") for z in range(2)])
            for z, s in enumerate(pairs.slots):
                s.free = scratch.slots[2 * z].free + scratch.slots[2 * z + 1].free
            E_ring = Ring([give(8 * P) for _ in range(2)])
            M_buf = Slot(rope_buf)
            V.wait([z.free for z in rope_tmp.slots])
            A_ring = Ring([give(P) for _ in range(2)])
            X_ring = Ring([give(P) for _ in range(1)])
            o, m_o = t1, [None] * 8
            A.wait(m_lt)
            A.wait(T.last())

            def decays(hd, t):
                pr = pairs.next()
                T.wait(pr.free, m_lt, m_c3)
                lt = lf_tm[:, t, hd * P:(hd + 1) * P]
                T.mm(pr.ap[:, 0:512], lt, decay[:, 0:4, :].rearrange("p l n -> p (l n)"))
                T.mm(pr.ap[:, 512:896], lt, decay[:, 4:7, :].rearrange("p l n -> p (l n)"))
                T.mm(pr.ap[:, 896:1024], lt, decay[:, 7 + t, :])
                m = T.mark()
                s = E_ring.next()
                m = a_act(s.ap, pr.ap, ACT.Exp, m, s.free)
                pr.free = [m]
                qt, kt = q[:, hd, t * P:(t + 1) * P], k[:, hd, t * P:(t + 1) * P]
                last = []
                for n in range(7):
                    bs = 1 << n
                    ev = s.ap[:, n * P:(n + 1) * P].rearrange("p (g r b) -> p g r b", r=2, b=bs)
                    q4 = qt.rearrange("p (g r b) -> p g r b", r=2, b=bs)
                    k4 = kt.rearrange("p (g r b) -> p g r b", r=2, b=bs)
                    last.append(v_tt(ev[:, :, 1, :], ev[:, :, 1, :], q4[:, :, 1, :], ALU.mult, m, m_q[hd // 2]))
                    last.append(v_tt(ev[:, :, 0, :], ev[:, :, 0, :], k4[:, :, 0, :], ALU.mult, m, m_k[hd // 2]))
                whole = s.ap[:, 7 * P:8 * P]
                last.append(v_tt(whole, whole, kt if t == 0 else qt, ALU.mult, m))
                return s, V.last()

            def pair_scores(hd, t, s, m_s):
                pr = pairs.next()
                T.wait(pr.free, m_s)
                for n in range(7):
                    e = s.ap[:, n * P:(n + 1) * P]
                    T.mm(pr.ap[:, n * P:(n + 1) * P], e, e)
                T.mm(pr.ap[:, 7 * P:8 * P], k[:, hd, t * P:(t + 1) * P], q[:, hd, t * P:(t + 1) * P])
                m = T.mark()
                m = v_tt(M_buf.ap, pr.ap, mask, ALU.mult, m, M_buf.free)
                pr.free = [m]
                ar = A_ring.next()
                m = V.do(lambda e: e.tensor_reduce(ar.ap, M_buf.ap.rearrange("p (l n) -> p n l", l=8), AX, ALU.add), m, ar.free)
                M_buf.free = [m]
                return ar, m

            prev = None
            for hd in range(NH + 1):
                cur = None
                if hd < NH:
                    es = [decays(hd, t) for t in range(TT)]
                if hd < NH:
                    ar0, ma0 = pair_scores(hd, 0, *es[0])
                    ar1, ma1 = pair_scores(hd, 1, *es[1])
                    b = proj.next()
                    T.wait(b.free)
                    T.mm(b.ap[:, 0:P], es[0][0].ap[:, 7 * P:8 * P], es[1][0].ap[:, 7 * P:8 * P])
                    m = T.mark()
                    es[0][0].free = [m]
                    es[1][0].free = [m]
                    xr = X_ring.next()
                    mx_ = a_copy(xr.ap, b.ap[:, 0:P], m, xr.free)
                    b.free = [mx_]
                    b = proj.next()
                    c = slice(hd * P, (hd + 1) * P)
                    T.wait(b.free, ma0, ma1, mx_, m_v)
                    T.mm(b.ap[:, 0:P], v[:, 0, c], ar0.ap)
                    T.mm(b.ap[:, P:S], v[:, 0, c], xr.ap, stop=False)
                    T.mm(b.ap[:, P:S], v[:, 1, c], ar1.ap, start=False)
                    m = T.mark()
                    ar0.free = ar1.free = xr.free = [m]
                    m_o[hd] = a_copy(o[:, hd, :], b.ap[:, 0:S], m)
                    b.free = [m_o[hd]]
                    pace(PACE_HEAD)
            for z, s in enumerate(pairs.slots):
                scratch.slots[2 * z].free = scratch.slots[2 * z + 1].free = s.free
            new_phase()
            give, tiles = carve()
            g, m_g = tiles(8), [None] * 8
            for j in range(4):
                b, m = project("hgrn_in", (12 + j,), h)
                m = a_act(flat(g[:, 2 * j:2 * j + 2, :]), b.ap, ACT.Silu, m)
                b.free = [m]
                m_g[2 * j] = m_g[2 * j + 1] = m
            head_norm(o, 8, 1, 1e-6, lambda n: col("hgrn_norm", n), (g, m_g), y_split, m_o)
            return "hgrn_out", y_split

        def diff():
            give, tiles = carve()
            q, k, v = tiles(8), tiles(8), tiles(TT, D)
            o, m_o = t1, [None] * 8
            m_q, m_k, m_v = [], [], []

            def q_piece(j):
                b, m = project("diff_in", (j,), h)
                m_q.append(rope(q[:, 2 * j:2 * j + 2, :], b, m, cos16, sin16, con("swap16"), m_rope, scale=64 ** -0.5))

            def k_piece(j):
                b, m = project("diff_in", (4 + j,), h)
                m_k.append(rope(k[:, 2 * j:2 * j + 2, :], b, m, cos16, sin16, con("swap16"), m_rope))

            def v_piece(j):
                to_tokens2("diff_in", v, 8, 1, m_v, j)

            q_piece(0)
            k_piece(0)
            v_piece(0)
            stats = small[:, 48:96]
            P_ring = Ring([give(2 * S) for _ in range(4)])
            PT_ring = Ring([give(S) for _ in range(3)])
            A.wait(h.marks, x_ready)
            V.wait(h.marks, x_ready)

            def scores(it, bank):
                hd, t, i = it
                nk = (t + 1) * P
                T.wait(m_q[hd // 2], m_k[hd // 2])
                for c in range(2):
                    if c:
                        T.wait(T.mark())
                    r = slice(64 * c, 64 * c + 64)
                    T.mm(bank.ap[:, c * S:c * S + nk], q[r, hd, t * P:(t + 1) * P], k[r, hd, 0:nk], stop=False)
                    T.mm(bank.ap[:, c * S + nk - P:c * S + nk], ident, con("mask_after"), start=False)
                return T.mark()

            def weigh(it, bank, m, slot):
                hd, t, i = it
                nk = (t + 1) * P
                c = 6 * (i % 8)
                nm, rs, ri = (stats[:, c + 2 * z:c + 2 * z + 2] for z in range(3))
                both = bank.ap.rearrange("p (c n) -> p c n", c=2)[:, :, 0:nk]
                m = V.do(lambda e: e.tensor_reduce(nm, both, AX, ALU.max, negate=True), m)
                w = slot.ap.rearrange("p (c n) -> p c n", c=2)
                for z in range(2):
                    me = a_act(w[:, z, 0:nk], both[:, z, :], ACT.Exp, m, slot.free, bias=nm[:, z:z + 1], accum=rs[:, z:z + 1])
                bank.free = [me]
                m = v_recip(ri, rs, me)
                m1 = v_tt(ri[:, 1:2], ri[:, 1:2], neg_lam, ALU.mult, m, m_nl)
                m2 = v_ts(w[:, 1, 0:nk], w[:, 1, 0:nk], ri[:, 1:2], None, ALU.mult, None, m1, me)
                return v_stt(w[:, 0, 0:nk], w[:, 0, 0:nk], ri[:, 0:1], w[:, 1, 0:nk], ALU.mult, ALU.add, m2)

            def values(it, bank, pt):
                hd, t, i = it
                c = slice(hd * P, (hd + 1) * P)
                T.wait(m_v)
                for b in range(t + 1):
                    T.mm(bank.ap[:, 0:P], v[:, b, c], pt[:, b * P:(b + 1) * P], start=(b == 0), stop=(b == t))
                m = T.mark()
                m_o[hd] = a_copy(o[:, hd, t * P:(t + 1) * P], bank.ap[:, 0:P], m)
                bank.free = [m_o[hd]]
                return m

            items = [(hd, t, 2 * hd + t) for hd in range(8) for t in range(TT)]
            between = {4 * j - 4 + z: (lambda f=f, j=j: f(j)) for j in range(1, 4) for z, f in enumerate((q_piece, k_piece, v_piece))}
            attend(items, scores, weigh, lambda it: it[1] + 1, values, P_ring, PT_ring, between)
            head_norm(o, 8, 1, 1e-6, lambda n: col("diff_norm"), None, y_split, m_o, more=1.0 - LAM_INIT)
            return "diff_out", y_split

        for i, mixer in enumerate((mlstm, swa, hgrn, diff)):
            g = 2 + i
            name, y = mixer()
            ada_until(g, 20)
            out_project(name, y, ToLayerNorm(scratch, i, 0, g, (g, 1)))
            ada_until(g)
            end = (g + 1, 8)
            ffn(h, "ffn_in", "ffn_out", i, False, ToLayerNorm(proj, i, 1, g, (g + 1, 0) if i < 3 else None), end)

        L.wait(*x_ready)
        L.steps.append((lambda e: e.dma_start(a["out"], flat(x)), s_out, 16))
        L.steps.append((None, s_out, 16))
        assert ada["n"] == len(todo)
        if plan is None:
            return wanted

        block = ctx.enter_context(nc.Block())

        @block.sync
        def _(eng):
            L.emit(eng)

        @block.tensor
        def _(eng):
            T.emit(eng)

        @block.vector
        def _(eng):
            V.emit(eng)

        @block.scalar
        def _(eng):
            A.emit(eng)

        @block.gpsimd
        def _(eng):
            G.emit(eng)
    return wanted


def _by_columns(w):
    k, n = w.shape
    return w.reshape(k // P, P, n // PC, PC).transpose(2, 1, 0, 3).reshape(n // PC, P, -1)


def _by_outputs(w):
    k, n = w.shape
    return w.T.reshape(n // PC, 2, P, k).transpose(0, 2, 1, 3).reshape(n // PC, P, -1)


def _by_rows(w):
    return w.reshape(-1, 2, P, D).transpose(0, 2, 1, 3).reshape(-1, P, 2 * D)


def _narrow(w, at):
    out = np.zeros((D, P), w[0].dtype)
    for a, c in zip(w, at):
        out[:, c:c + a.shape[1]] = a
    return out.reshape(KT, P, P).transpose(1, 0, 2).reshape(P, -1)


def lay_out(v):
    st = lambda f, xs: np.ascontiguousarray(np.stack([f(z) for z in xs]))
    one = lambda z: np.ascontiguousarray(z)
    out = {}
    out["x"] = one(v["x"][0].T.reshape(KT, P, S).transpose(1, 0, 2).reshape(P, -1))
    out["c_rows"] = one(np.broadcast_to(v["c"], (P, D)))
    out["c_rows2"] = one(np.broadcast_to(v["c_2"], (P, D)))
    out["w_ada"] = st(_by_outputs, v["w_ada"])
    out["ada_w_2"] = st(lambda w: np.concatenate([_by_outputs(w[0]), _by_outputs(w[1])]), v["ada_w_2"])
    cut = np.cumsum([512, 512, 512, 512, 256, 256, 512, 16, 512, 512, 512, 512, 4])
    sec = lambda w, i: w[:, (cut[i - 1] if i else 0):cut[i]]
    out["w_in"] = st(lambda w: _by_columns(np.concatenate([w[:, 0:cut[6]], w[:, cut[7]:cut[11]]], 1)), v["w_in"])
    out["w_in_s"] = st(lambda w: _narrow((sec(w, 12), sec(w, 7)), (0, 32)), v["w_in"])
    out["w_mg"] = st(_by_columns, v["w_mg"])
    out["w_br"] = st(lambda w: np.stack([_by_columns(z) for z in w]), v["w_br"])
    for n in ("w_o", "w_up"):
        out[n] = st(_by_columns, v[n])
    out["w_down"] = st(_by_rows, v["w_down"])
    mi = v["mlstm_w_in_2"][0]
    out["mlstm_in"] = one(_by_columns(mi[:, 0:3072]))
    out["mlstm_in_s"] = one(_narrow((mi[:, 3072:3076], mi[:, 3076:3080]), (0, 32))[None])
    for a_, b_ in (("swa_in", "swa_w_in_2"), ("hgrn_in", "hgrn_w_in_2"), ("diff_in", "diff_w_in_2"),
                   ("mlstm_out", "mlstm_w_out_2"), ("swa_out", "swa_w_out_2"), ("hgrn_out", "hgrn_w_out_2"), ("diff_out", "diff_w_out_2")):
        out[a_] = one(_by_columns(v[b_][0]))
    out["ffn_in"] = st(_by_columns, v["ffn_w_in_2"])
    out["ffn_out"] = st(_by_rows, v["ffn_w_out_2"])
    for l in range(2):
        out[f"wa2{l}"] = one(np.concatenate([v["w_gla_a2"][l], v["b_gla_a"][l][None]], 0))
    out["sinks"] = one(v["swa_sinks_2"].reshape(1, 16))
    out["lam"] = one(v["diff_lambda_2"].reshape(1, 256))
    out["pos"] = one(v["positions_2"].reshape(1, S))
    c = np.zeros((P, N_COLS), v["x"].dtype)

    def put(name, vec):
        at, n = COLS[name]
        c[:, at:at + n] = vec.reshape(n, P).T

    for l in range(2):
        for n in ("norm1_g", "norm2_g", "b_ada", "ret_norm_g", "gla_norm_g", "q_norm_g", "k_norm_g", "b_mg", "w_conv", "b_conv"):
            put(f"{n}{l}", v[n][l])
        c[0:4, COLS[f"b_fox_f{l}"][0]] = v["b_fox_f"][l]
    for i in range(4):
        put(f"ada_b_2{i}", v["ada_b_2"][i])
        put(f"ln_g_2{i}", v["ln_g_2"][i])
        put(f"ln_b_2{i}", v["ln_b_2"][i])
    put("mlstm_norm", v["mlstm_norm_2"][0])
    c[0:4, COLS["b_gate"][0]] = v["mlstm_b_gate_2"][0][0:4]
    c[32:36, COLS["b_gate"][0]] = v["mlstm_b_gate_2"][0][4:8]
    put("hgrn_lb", v["hgrn_lower_bounds_2"])
    put("hgrn_norm", v["hgrn_norm_2"][0])
    put("diff_norm", v["diff_norm_2"][0])
    out["cols"] = c
    return out


def kernel(**inputs):
    import concourse.bacc as bacc
    from concourse.bass_utils import run_bass_kernel_spmd

    arrays = lay_out({n: np.asarray(z) for n, z in inputs.items()})
    where = []
    for name, part in zip(("const0", "const1", "const3"), constants()):
        arrays[name], at = _join(part)
        where.append(at)

    def fresh():
        nc = bacc.Bacc("TRN2", target_bir_lowering=False, num_devices=1)
        aps = {n: nc.dram_tensor(f"in_{n}", z.shape, mybir.dt.from_np(z.dtype), kind="ExternalInput").ap()
               for n, z in arrays.items()}
        aps["out"] = nc.dram_tensor("out_x", [P, KT * S], F32, kind="ExternalOutput").ap()
        return nc, aps

    plan = build(*fresh(), None, where)
    nc, aps = fresh()
    build(nc, aps, plan, where)
    r = run_bass_kernel_spmd(nc, [{f"in_{n}": z for n, z in arrays.items()}], core_ids=[0])
    got = r.results[0]["out_x"]
    return got.reshape(P, KT, S).transpose(2, 1, 0).reshape(1, S, D)
```
